# Optimizing a Trainium2 kernel written in Bass

```python
import math
import jax, jax.numpy as jnp
from jax import lax
import numpy as np

D_MODEL = 1024
BATCH = 1
SEQ = 512
DEPTH = 1

CHUNK = 64
NORM_EPS = 1e-6
GDN_HEADS = 8
GDN_DK = 128
GDN_DV = 128
GDN_CONV = 4
MLA_HEADS = 8
MLA_Q_LORA = 512
MLA_KV_LORA = 256
MLA_NOPE = 128
MLA_ROPE = 64
MLA_V = 128
ROPE_THETA = 10000.0
Q_BLOCK = 128
N_EXPERTS = 32
TOP_K = 4
D_EXPERT = 1024
SWIGLU_LIMIT = 7.0
SWIGLU_ALPHA = 1.702
MOE_BLOCK = 128

GDN_QK_W = GDN_HEADS * GDN_DK
GDN_V_W = GDN_HEADS * GDN_DV
GDN_CONV_W = 2 * GDN_QK_W + GDN_V_W
COL_SIZES = (GDN_QK_W, GDN_QK_W, GDN_V_W, GDN_V_W, GDN_HEADS, GDN_HEADS,
             MLA_Q_LORA, MLA_KV_LORA + MLA_ROPE, D_MODEL, D_MODEL)
IN_COLS = sum(COL_SIZES)
COL_SPLITS = tuple(int(c) for c in np.cumsum(COL_SIZES)[:-1])

kernel_name = 'hybrid_gdn_mla_moe_block'

def rmsnorm(x, w):
    xf = x.astype(jnp.float32)
    xf = xf * lax.rsqrt(jnp.mean(xf * xf, axis=-1, keepdims=True) + NORM_EPS)
    return (xf * w.astype(jnp.float32)).astype(x.dtype)

def l2norm(x):
    xf = x.astype(jnp.float32)
    return xf * lax.rsqrt(jnp.sum(xf * xf, axis=-1, keepdims=True) + NORM_EPS)

def causal_depthwise_conv(x, w):
    k_taps, c = w.shape
    return lax.conv_general_dilated(
        x, w[:, None, :].astype(x.dtype), window_strides=(1,),
        padding=[(k_taps - 1, 0)], dimension_numbers=('NWC', 'WIO', 'NWC'),
        feature_group_count=c)

def to_chunks(t):
    b, s, h = t.shape[:3]
    t = t.reshape((b, s // CHUNK, CHUNK, h) + t.shape[3:])
    return jnp.moveaxis(t, 3, 1)

def gated_delta_rule(q, k, v, g, beta):
    b, s, h, dk = q.shape
    dv = v.shape[-1]
    qc, kc, vc = to_chunks(q), to_chunks(k), to_chunks(v)
    gc = jnp.cumsum(to_chunks(g), axis=-1)
    bc = to_chunks(beta)[..., None]
    idx = jnp.arange(CHUNK)
    incl = idx[:, None] >= idx[None, :]
    strict = idx[:, None] > idx[None, :]
    decay = jnp.exp(jnp.where(incl, gc[..., :, None] - gc[..., None, :], -jnp.inf))
    kb = kc * bc
    lower = jnp.where(strict, jnp.einsum('bhnck,bhnmk->bhncm', kb, kc) * decay, 0.0)
    a_mat = jnp.eye(CHUNK, dtype=jnp.float32) + lower
    u = lax.linalg.triangular_solve(a_mat, vc * bc, left_side=True, lower=True)
    w = lax.linalg.triangular_solve(a_mat, kb * jnp.exp(gc)[..., None], left_side=True, lower=True)
    qk = jnp.where(incl, jnp.einsum('bhnck,bhnmk->bhncm', qc, kc) * decay, 0.0)
    q_dec = qc * jnp.exp(gc)[..., None]
    k_dec = kc * jnp.exp(gc[..., -1:] - gc)[..., None]
    g_last = jnp.exp(gc[..., -1])

    def step(state, inp):
        u_i, w_i, qk_i, qd_i, kd_i, gl_i = inp
        v_new = u_i - jnp.einsum('bhck,bhkv->bhcv', w_i, state)
        o_i = jnp.einsum('bhck,bhkv->bhcv', qd_i, state) + jnp.einsum('bhcm,bhmv->bhcv', qk_i, v_new)
        state = state * gl_i[..., None, None] + jnp.einsum('bhck,bhcv->bhkv', kd_i, v_new)
        return state, o_i

    xs = tuple(jnp.moveaxis(t, 2, 0) for t in (u, w, qk, q_dec, k_dec, g_last))
    state0 = jnp.zeros((b, h, dk, dv), jnp.float32)
    _, o = lax.scan(step, state0, xs)
    return jnp.transpose(o, (1, 0, 3, 2, 4)).reshape(b, s, h, dv)

def rope_tables(s):
    inv = 1.0 / (ROPE_THETA ** (jnp.arange(0, MLA_ROPE, 2, dtype=jnp.float32) / MLA_ROPE))
    ang = jnp.arange(s, dtype=jnp.float32)[:, None] * inv[None, :]
    ang = jnp.concatenate([ang, ang], axis=-1)
    return jnp.cos(ang), jnp.sin(ang)

def apply_rope(x, cos, sin):
    shape = (x.shape[1],) + (1,) * (x.ndim - 3) + (x.shape[-1],)
    xf = x.astype(jnp.float32)
    half = x.shape[-1] // 2
    rot = jnp.concatenate([-xf[..., half:], xf[..., :half]], axis=-1)
    return (xf * cos.reshape(shape) + rot * sin.reshape(shape)).astype(x.dtype)

def chunk_causal_attention(q, k, v):
    b, s, h, dqk = q.shape
    n_blocks = s // Q_BLOCK
    scale = dqk ** -0.5
    k_chunk = jnp.arange(s) // CHUNK

    def one_block(i):
        start = i * Q_BLOCK
        qb = lax.dynamic_slice_in_dim(q, start, Q_BLOCK, axis=1)
        sc = jnp.einsum('bqhd,bkhd->bhqk', qb, k, preferred_element_type=jnp.float32) * scale
        q_chunk = (start + jnp.arange(Q_BLOCK)) // CHUNK
        mask = k_chunk[None, :] <= q_chunk[:, None]
        p = jax.nn.softmax(jnp.where(mask, sc, -jnp.inf), axis=-1).astype(v.dtype)
        return jnp.einsum('bhqk,bkhd->bqhd', p, v)

    o = lax.map(one_block, jnp.arange(n_blocks))
    return jnp.moveaxis(o, 0, 1).reshape(b, s, h, v.shape[-1])

def hybrid_mixer(h, cos, sin, w_in, gdn_conv_w, gdn_a_log, gdn_dt_bias, gdn_norm_w, w_gdn_o,
                 mla_q_norm_w, w_mla_q_b, mla_kv_norm_w, w_mla_kv_b, w_mla_o, w_out):
    b, s, _ = h.shape
    f32 = jnp.float32
    proj = jnp.einsum('bsd,de->bse', h, w_in)
    q_g, k_g, v_g, z_g, b_g, a_g, c_q, c_kv, gate_a, gate_b = jnp.split(proj, COL_SPLITS, axis=-1)

    qkv = jax.nn.silu(causal_depthwise_conv(jnp.concatenate([q_g, k_g, v_g], axis=-1), gdn_conv_w))
    q_g, k_g, v_g = jnp.split(qkv, (GDN_QK_W, 2 * GDN_QK_W), axis=-1)
    q_g = l2norm(q_g.reshape(b, s, GDN_HEADS, GDN_DK)) * (GDN_DK ** -0.5)
    k_g = l2norm(k_g.reshape(b, s, GDN_HEADS, GDN_DK))
    v_g = v_g.reshape(b, s, GDN_HEADS, GDN_DV).astype(f32)
    beta = jax.nn.sigmoid(b_g.astype(f32))
    g = -jnp.exp(gdn_a_log.astype(f32)) * jax.nn.softplus(a_g.astype(f32) + gdn_dt_bias.astype(f32))
    o_a = gated_delta_rule(q_g, k_g, v_g, g, beta)
    o_a = rmsnorm(o_a, gdn_norm_w) * jax.nn.silu(z_g.reshape(b, s, GDN_HEADS, GDN_DV).astype(f32))
    y_a = jnp.einsum('bse,ed->bsd', o_a.reshape(b, s, GDN_V_W).astype(h.dtype), w_gdn_o)

    q = jnp.einsum('bsr,re->bse', rmsnorm(c_q, mla_q_norm_w), w_mla_q_b)
    q = q.reshape(b, s, MLA_HEADS, MLA_NOPE + MLA_ROPE)
    q_nope, q_rope = q[..., :MLA_NOPE], apply_rope(q[..., MLA_NOPE:], cos, sin)
    kv_lat = rmsnorm(c_kv[..., :MLA_KV_LORA], mla_kv_norm_w)
    k_rope = apply_rope(c_kv[..., MLA_KV_LORA:], cos, sin)
    kv = jnp.einsum('bsr,re->bse', kv_lat, w_mla_kv_b).reshape(b, s, MLA_HEADS, MLA_NOPE + MLA_V)
    k_nope, v = kv[..., :MLA_NOPE], kv[..., MLA_NOPE:]
    q_full = jnp.concatenate([q_nope, q_rope], axis=-1)
    k_full = jnp.concatenate([k_nope, jnp.broadcast_to(k_rope[:, :, None, :], (b, s, MLA_HEADS, MLA_ROPE))], axis=-1)
    o_b = chunk_causal_attention(q_full, k_full, v)
    y_b = jnp.einsum('bse,ed->bsd', o_b.reshape(b, s, MLA_HEADS * MLA_V), w_mla_o)

    merged = jax.nn.sigmoid(gate_a) * y_a + jax.nn.sigmoid(gate_b) * y_b
    return jnp.einsum('bsd,de->bse', merged, w_out)

def moe_ffn(h, w_router, b_router, w_gate_up, b_gate_up, w_down, b_down):
    b, s, d = h.shape
    f32 = jnp.float32
    n_tok = b * s
    hf = h.reshape(n_tok, d)
    logits = (hf @ w_router).astype(f32) + b_router.astype(f32)
    top_logits, top_idx = lax.top_k(logits, TOP_K)
    top_w = jax.nn.softmax(top_logits, axis=-1)
    n_assign = n_tok * TOP_K
    flat_e = top_idx.reshape(-1)
    order = jnp.argsort(flat_e)
    sorted_e = flat_e[order]
    counts = jnp.bincount(flat_e, length=N_EXPERTS)
    start = jnp.cumsum(counts) - counts
    padded = (counts + MOE_BLOCK - 1) // MOE_BLOCK * MOE_BLOCK
    pad_end = jnp.cumsum(padded)
    pad_start = pad_end - padded
    dest = pad_start[sorted_e] + jnp.arange(n_assign) - start[sorted_e]
    n_pad = n_assign + N_EXPERTS * MOE_BLOCK
    n_blocks = n_pad // MOE_BLOCK
    slot_tok = jnp.zeros((n_pad,), jnp.int32).at[dest].set((order // TOP_K).astype(jnp.int32))
    slot_w = jnp.zeros((n_pad,), f32).at[dest].set(top_w.reshape(-1)[order])
    block_e = jnp.minimum(jnp.searchsorted(pad_end, jnp.arange(n_blocks) * MOE_BLOCK, side='right'), N_EXPERTS - 1)
    xs = hf[slot_tok].reshape(n_blocks, MOE_BLOCK, d)

    def expert_block(args):
        xb, e = args
        gu = xb @ w_gate_up[e] + b_gate_up[e]
        gate = jnp.minimum(gu[:, ::2], SWIGLU_LIMIT)
        up = jnp.clip(gu[:, 1::2], -SWIGLU_LIMIT, SWIGLU_LIMIT)
        act = (up + 1.0) * (gate * jax.nn.sigmoid(gate * SWIGLU_ALPHA))
        return act @ w_down[e] + b_down[e]

    ys = lax.map(expert_block, (xs, block_e)).reshape(n_pad, d)
    y = jax.ops.segment_sum(ys.astype(f32) * slot_w[:, None], slot_tok, num_segments=n_tok)
    return y.astype(h.dtype).reshape(b, s, d)

def setup_inputs(seed: int = 0) -> dict:
    key = jax.random.key(seed)
    ks = iter(jax.random.split(key, 24))
    f32 = jnp.float32

    def nrm(shape, scale):
        return jax.random.normal(next(ks), shape, f32) * scale

    L = DEPTH
    x = nrm((BATCH, SEQ, D_MODEL), 1.0)
    norm_mix_w = 1.0 + nrm((L, D_MODEL), 0.05)
    w_in = nrm((L, D_MODEL, IN_COLS), D_MODEL ** -0.5)
    gdn_conv_w = nrm((L, GDN_CONV, GDN_CONV_W), GDN_CONV ** -0.5)
    gdn_a_log = jnp.log(jax.random.uniform(next(ks), (L, GDN_HEADS), f32, 1.0, 16.0))
    dt = jnp.exp(jax.random.uniform(next(ks), (L, GDN_HEADS), f32, math.log(1e-3), math.log(1e-1)))
    gdn_dt_bias = dt + jnp.log(-jnp.expm1(-dt))
    gdn_norm_w = 1.0 + nrm((L, GDN_DV), 0.05)
    w_gdn_o = nrm((L, GDN_V_W, D_MODEL), GDN_V_W ** -0.5)
    mla_q_norm_w = 1.0 + nrm((L, MLA_Q_LORA), 0.05)
    w_mla_q_b = nrm((L, MLA_Q_LORA, MLA_HEADS * (MLA_NOPE + MLA_ROPE)), MLA_Q_LORA ** -0.5)
    mla_kv_norm_w = 1.0 + nrm((L, MLA_KV_LORA), 0.05)
    w_mla_kv_b = nrm((L, MLA_KV_LORA, MLA_HEADS * (MLA_NOPE + MLA_V)), MLA_KV_LORA ** -0.5)
    w_mla_o = nrm((L, MLA_HEADS * MLA_V, D_MODEL), (MLA_HEADS * MLA_V) ** -0.5)
    w_out = nrm((L, D_MODEL, D_MODEL), D_MODEL ** -0.5)
    norm_ffn_w = 1.0 + nrm((L, D_MODEL), 0.05)
    w_router = nrm((L, D_MODEL, N_EXPERTS), D_MODEL ** -0.5)
    b_router = nrm((L, N_EXPERTS), 0.01)
    w_gate_up = nrm((L, N_EXPERTS, D_MODEL, 2 * D_EXPERT), D_MODEL ** -0.5)
    b_gate_up = nrm((L, N_EXPERTS, 2 * D_EXPERT), 0.01)
    w_down = nrm((L, N_EXPERTS, D_EXPERT, D_MODEL), D_EXPERT ** -0.5)
    b_down = nrm((L, N_EXPERTS, D_MODEL), 0.01)
    norm_final_w = 1.0 + nrm((D_MODEL,), 0.05)
    return {'x': x, 'norm_mix_w': norm_mix_w, 'w_in': w_in, 'gdn_conv_w': gdn_conv_w,
            'gdn_a_log': gdn_a_log, 'gdn_dt_bias': gdn_dt_bias, 'gdn_norm_w': gdn_norm_w,
            'w_gdn_o': w_gdn_o, 'mla_q_norm_w': mla_q_norm_w, 'w_mla_q_b': w_mla_q_b,
            'mla_kv_norm_w': mla_kv_norm_w, 'w_mla_kv_b': w_mla_kv_b, 'w_mla_o': w_mla_o,
            'w_out': w_out, 'norm_ffn_w': norm_ffn_w, 'w_router': w_router, 'b_router': b_router,
            'w_gate_up': w_gate_up, 'b_gate_up': b_gate_up, 'w_down': w_down, 'b_down': b_down,
            'norm_final_w': norm_final_w}

def reference(x, norm_mix_w, w_in, gdn_conv_w, gdn_a_log, gdn_dt_bias, gdn_norm_w, w_gdn_o,
              mla_q_norm_w, w_mla_q_b, mla_kv_norm_w, w_mla_kv_b, w_mla_o, w_out,
              norm_ffn_w, w_router, b_router, w_gate_up, b_gate_up, w_down, b_down, norm_final_w):
    cos, sin = rope_tables(x.shape[1])
    for layer in range(DEPTH):
        h = rmsnorm(x, norm_mix_w[layer])
        x = x + hybrid_mixer(h, cos, sin, w_in[layer], gdn_conv_w[layer], gdn_a_log[layer],
                             gdn_dt_bias[layer], gdn_norm_w[layer], w_gdn_o[layer],
                             mla_q_norm_w[layer], w_mla_q_b[layer], mla_kv_norm_w[layer],
                             w_mla_kv_b[layer], w_mla_o[layer], w_out[layer])
        h = rmsnorm(x, norm_ffn_w[layer])
        x = x + moe_ffn(h, w_router[layer], b_router[layer], w_gate_up[layer], b_gate_up[layer],
                        w_down[layer], b_down[layer])
    return rmsnorm(x, norm_final_w)


_drawn_inputs = setup_inputs


def setup_inputs(seed=0):
    import zlib

    import numpy as np

    out = dict(_drawn_inputs(seed))
    spreads = {}
    factors = {'mla_q_norm_w': 3.111, 'b_gate_up': 8.0, 'b_down': 8.0}
    for name, (base, spread) in spreads.items():
        noise = np.random.default_rng([zlib.crc32(name.encode()), seed]).standard_normal(out[name].shape)
        drawn = base * np.exp(spread * noise) if base else spread * noise
        out[name] = __import__('jax').numpy.asarray(drawn.astype(out[name].dtype))
    for name, factor in factors.items():
        out[name] = (out[name] * factor).astype(out[name].dtype)
    return out
```

```python
from contextlib import ExitStack

import numpy as np
import concourse.bass as bass
from concourse import mybir

ALU = mybir.AluOpType
ACT = mybir.ActivationFunctionType
AXX = mybir.AxisListType.X
F32 = mybir.dt.float32
BF16 = mybir.dt.bfloat16
I32 = mybir.dt.int32
U32 = mybir.dt.uint32

P = 128
SEQ = 512
D = 1024
NT = SEQ // P
KD = D // P
CHUNK = 64
HEADS = 8
PAIRS = HEADS // 2
Q_LORA, KV_LORA, ROPE = 512, 256, 64
KQ, KKV = Q_LORA // P, KV_LORA // P
EPS = 1e-6
ATT_SCALE = (128 + ROPE) ** -0.5
GDN_SCALE = 128 ** -0.5
NE, TOPK, DE = 32, 4, 1024
LIMIT, ALPHA = 7.0, 1.702
MAX_EXTRA = (SEQ * TOPK - 1) // P
FAR = 1 << 20
NEG = -1.0e30
LEVELS = [1, 2, 4, 8, 16, 32]
NC = SEQ // CHUNK
UNITS = 2 * NT
SCAN_SLOTS = UNITS + 2 - (len(LEVELS) - 1)

M_INCL, M_SAME, M_ONES, M_IND0, M_IND1, M_ID, M_BEFORE, M_LEVEL = 0, 1, 2, 3, 4, 5, 6, 7
N_MASKS = M_LEVEL + len(LEVELS)

F_G, F_GC, F_BETA, F_BEG, F_EKD, F_GL0, F_GL1 = range(7)
NF = 7

REGION = {"A": (0, 2), "B": (2, 2), "C": (4, 2), "D": (6, 1), "E": (7, 1)}


def slot_fills(n):
    f = [(f"sc{n}", "D", 1)] if n < UNITS else []
    f += [(f"pt{n - 1}", "E", 1)] if 1 <= n <= UNITS else []
    f += [(f"pv{n - 2}", "E", 1)] if 2 <= n else []
    return f


def pair_fills():
    f = [("q0", "A", 1), ("q1", "A", 1), ("k0", "B", 1), ("ss0", "D", 0), ("k1", "B", 1), ("ss1", "D", 0),
         ("v0", "C", 1), ("ss2", "D", 0), ("v1", "C", 1), ("z", "A", 1), ("ss3", "D", 1),
         ("kt", "B", 1), ("vt", "C", 1), ("qr", "E", 2), ("qn", "A", 1), ("kn", "C", 1),
         ("rg", "B", 2), ("ra", "A", 1), ("kk0", "D", 1), ("kk1", "E", 1), ("rb", "C", 1), ("qk", "B", 1),
         ("va", "A", 1), ("t1_0", "D", 1), ("t1_1", "E", 1)]
    for n, s in enumerate(LEVELS[1:]):
        f += [(f"x{s}", "A", 1)] + slot_fills(n)
        f += [] if s == LEVELS[-1] else [(f"tx{s}", "B", 1)]
        f += [(f"tr{s}", "C", 1)]
    f += [("wt", "A", 1), ("u", "B", 1)]
    for c in range(NC):
        f += [(f"ws{c}", "A", 0)] + (slot_fills(len(LEVELS) - 1 + c) if c < SCAN_SLOTS else [])
        f += [(f"ds{c}", "A", 1), (f"o{c}", "BC"[c % 2], 1)]
    f += [("ot0", "D", 1), ("ot1", "E", 1)]
    return f


PRE = ([(f"h{k}", "ABCDE"[k % 5], 1) for k in range(KD)]
       + [("ba", "A", 1), ("cq0", "B", 1), ("gs", "C", 1), ("cq1", "D", 1), ("cq2", "E", 1), ("cq3", "A", 1)]
       + [(f"kv{j}", "CD"[j], 1) for j in range(KKV)]
       + [("kr", "B", 2), ("cqs", "C", 1), ("kvs", "D", 1)])
PAIR = pair_fills()
MERGE = [("g0", "A", 1), ("y0", "B", 1), ("g1", "C", 1), ("ya1", "D", 1), ("yb1", "E", 1)]
OUT = ([(f"x{t}", "ABC"[t % 3], 1) for t in range(NT)]
       + [(f"r{k}", "DE"[k % 2], 1) for k in range(KD)]
       + [("lg", "A", 1), ("lt", "B", 1), ("pos", "C", 1), ("tot", "D", 1), ("ex", "E", 1), ("li", "A", 1)])


class Fills:

    def __init__(self, fills, before=None):
        self.base = before.base + before.n * before.turns if before else 0
        self.free_base = {r: before.free_at(r, before.turns) for r in REGION} if before else dict.fromkeys(REGION, 0)
        self.fills, self.n, self.turns = fills, len(fills), 1
        self.index = {name: j for j, (name, _, _) in enumerate(fills)}
        self.region = {name: r for name, r, _ in fills}
        self.per_turn = {r: sum(fr for _, q, fr in fills if q == r) for r in REGION}

    def times(self, turns):
        self.turns = turns
        return self

    def at(self, name, turn=0):
        return turn * self.n + (self.base + self.index[name] + 1)

    def free_at(self, region, turn=0):
        return turn * self.per_turn[region] + self.free_base[region]

    def free_before(self, name, turn=0):
        r = self.region[name]
        return self.free_at(r, turn) + sum(fr for m, q, fr in self.fills[:self.index[name]] if q == r)


PRE_F = Fills(PRE)
PAIR_F = Fills(PAIR, PRE_F).times(PAIRS)
MERGE_F = Fills(MERGE, PAIR_F).times(KD // 2)
OUT_F = Fills(OUT, MERGE_F)


def build(nc, x, norm_mix, w_ba, a_log, dt_bias, w_cq, w_ckv, q_norm, kv_norm, w_pair, conv_w, w_qb, w_kvb,
          gdn_norm, w_merge, w_out, norm_ffn, w_router, b_router, w_gu, b_gu, w_dn, b_dn, norm_final,
          masks, diag, cos, sin, small, ints, out):
    ctx = ExitStack()
    with ctx:
        def sb(name, shape, dt=F32):
            return ctx.enter_context(nc.sbuf_tensor(name, shape, dt))

        def sem(name):
            return ctx.enter_context(nc.semaphore(name))

        h2_dram = nc.dram_tensor("h2_rows", [SEQ, D], F32, kind="Internal").ap()
        slot_dram = nc.dram_tensor("slot_table", [P * P, 1], I32, kind="Internal").ap()
        y_dram = nc.dram_tensor("expert_rows", [SEQ * TOPK, D], F32, kind="Internal").ap()
        bias_dram = nc.dram_tensor("bias_parts", [NE, 3, 3 * DE], BF16, kind="Internal").ap()

        mk = sb("mk", [P, N_MASKS, P])
        dg = sb("dg", [P, P])
        csn = sb("csn", [P, 2, SEQ])
        hT = sb("hT", [P, KD, SEQ])
        oaT = sb("oaT", [P, HEADS, SEQ])
        obT = sb("obT", [P, HEADS, SEQ])
        fac = sb("fac", [P, HEADS, NF, NT])
        gw = sb("gw", [P, P])
        cw = sb("cw", [P, PAIRS, 24])
        taps = sb("taps", [P, 6, 4])
        fcur = sb("fcur", [P, 2, NF, NT])
        nw = sb("nw", [P, KD + KQ + KKV])
        gp = sb("gp", [P, 16])
        sm = sb("sm", [P, 3 * 32 + 16])
        thr = sb("thr", [32, 16])
        wr = sb("wr", [P, KD, NE])
        br = sb("br", [P, NE])
        valt = sb("valt", [P, NT * TOPK], I32)
        r4 = sb("r4", [P, 2, NT])
        gmt = sb("gmt", [P, 6, NT, HEADS])
        r16 = sb("r16", [P, 16])
        lf = sb("lf", [P, 4, 2, NT])
        r8 = sb("r8", [P, 8])
        nm = sb("nm", [P, 3, UNITS])
        lst = sb("lst", [1, 40], I32)
        tab = sb("tab", [P, P], I32)
        tok = sb("tok", [P, P], I32)
        gix = sb("gix", [P, 1], I32)
        six = sb("six", [P, 1], I32)
        w4 = sb("w4", [P, NT, TOPK])
        ones3 = sb("ones3", [3, P], BF16)

        K1 = 1024
        W = sb("arena", [P, 34 * K1 + 512])

        def ar(a, n, p=P):
            return W[0:p, int(a * K1):int(a * K1) + n]

        def ar3(a, b, c, p=P):
            return ar(a, b * c, p).rearrange("p (b c) -> p b c", b=b)

        cqn, kvn, krp = ar3(0, KQ, SEQ), ar3(2, KKV, SEQ), ar3(3, 2, SEQ)
        wqkvz = [ar3(4 + 2 * n, KD, 256) for n in range(4)]
        wqb, wkb = ar3(12, KQ, 384), ar3(13.5, KKV, 512)
        qn, qr, rot, kn, va = ar3(14.5, 2, SEQ), ar(15.5, SEQ), ar(16, SEQ), ar3(16.5, 2, SEQ), ar3(17.5, NT, 256)
        pb, ptb = ar3(18.5, 2, SEQ), ar3(19.5, 2, SEQ)
        qkvT = ar3(20.5, 6, SEQ)
        cv, sq = ar3(23.5, 2, SEQ), ar3(24.5, 2, SEQ)
        qT, kT, vT = (qkvT[:, 2 * n:2 * n + 2, :] for n in range(3))

        def units(a):
            return ar3(a, 2 * NT, P)

        kbg, kd, vb = units(25.5), units(26.5), units(27.5)
        sg, sa, sbq = units(28.5), units(29.5), units(30.5)
        qk = units(31.5)
        vnew = ar(32.5, 512).rearrange("p (a h d) -> p a h d", a=2, h=2)
        state = ar(33, 512).rearrange("p (a h d) -> p a h d", a=2, h=2)
        zs = ar3(33.5, NT, 256)
        dt_, lt_, cm = units(23.5), units(22.5), units(24.5)
        T, R, X = sg, sa, sbq
        er = units(18.5)
        WT, U = units(23.5), units(28.5)
        osb = ar(30.5, K1).rearrange("p (t h d) -> p t h d", t=NT, h=2)

        xin, wcq, wckv, wba = ar3(20.5, NT, D), ar3(24.5, KD, Q_LORA), ar3(28.5, KD, 384), ar3(31.5, KD, 16)
        csq, ksq, inv = ar3(18.5, KQ, SEQ), ar3(17.5, KKV, SEQ), ar3(16.5, 2, SEQ)

        mw = [ar(4 * b, 4 * K1).rearrange("p (w k m) -> p w k m", w=4, k=KD) for b in range(2)]
        gs_, mm_ = [ar3(8 + b, 2, SEQ) for b in range(2)], ar3(10, 2, SEQ)
        mT = ar3(12, KD, SEQ)
        wo = ar(16, 8 * K1).rearrange("p (h k n) -> p h k n", h=2, k=KD)
        x2 = ar3(24, NT, D)
        h2 = oaT[:, :, :].rearrange("p h s -> p (h s)").rearrange("p (t d) -> p t d", t=NT)
        h2T = obT
        hflat = hT[:, :, :].rearrange("p k s -> p (k s)")
        junk, nrow, ys = hflat[:, 0:D], hflat[:, D:2 * D], hflat[:, 2 * D:3 * D]
        bcur = ar(33, 3 * DE // 2, 3).bitcast(BF16)
        bfull, bpart = ar(28, 3 * DE, NE), ar(31, 3 * DE // 2, NE).bitcast(BF16)
        lgT = ar(28, SEQ, NE)
        rt = 29
        lg, mx8, ix8 = ar3(rt, NT, NE), ar3(rt + .25, NT, 8), ar3(rt + .375, NT, 8).bitcast(U32)
        ixf, e4, sum4, msk = ar3(rt + .5, NT, 4), ar3(rt + .5625, NT, 4), ar(rt + .625, 8), ar3(rt + .75, NT, NE)
        oh, adr, bb = ar3(rt + 1, 16, NE), ar3(rt + 1.5, NT, NE), ar3(rt + 1.75, NT, NE)
        pk, a16, a16i = ar3(rt + 2, 16, NE), ar(rt + 2.5, 16), ar(rt + 2.625, 16).bitcast(I32)
        cnt, fl, tot, rk = (ar(rt + 3 + n / 16, 4, NE) for n in range(4))
        oj, ol, lsf = ar(rt + 3.5, 48, NE), ar(rt + 3.75, 97, NE), ar(rt + 3.875, 40, 1)

        ring = [ar(2 * c, 2 * K1) for c in range(12)]
        xg, xT = ar(28, D), ar3(29, KD, P)
        gb, ub, sgm = ar(30, 512), ar(30.5, 512), ar(31, 512)
        act, aT = ar3(31.5, 2, 512), hflat[:, 3 * D:4 * D].rearrange("p (k m) -> p k m", k=KD)
        yin = [ar(5 * b, 4 * D).rearrange("p (k d) -> p k d", k=TOPK) for b in range(NT)]

        ps = ctx.enter_context(nc.psum_tensor("ps", [P, 8 * 512], F32))

        def region(r, n=1024):
            b = REGION[r][0] * 512
            return ps[:, b:b + n]

        yd = ps[:, 6 * 512:8 * 512].rearrange("p (h s) -> p h s", h=2)

        def two(r):
            return region(r).rearrange("p (h s) -> p h s", h=2)

        filled = sem("filled")
        region_free = {r: sem("region_free_" + r) for r in REGION}
        const_in, x_in, w_ba_in, w_cq_in, w_ckv_in = (sem(n) for n in ("const_in", "x_in", "w_ba_in", "w_cq_in", "w_ckv_in"))
        w_in = [sem(f"w_in_{n}") for n in "qkvz"]
        w_qb_in, w_kvb_in = sem("w_qb_in"), sem("w_kvb_in")
        ssx_done, rstd_done, xn_done, hT_done = (sem(n) for n in ("ssx_done", "rstd_done", "xn_done", "hT_done"))
        pre_step, pre_act, g_done, fac_done = (sem(n) for n in ("pre_step", "pre_act", "g_done", "fac_done"))
        lat_raw = sem("lat_raw")
        lat_sq, lat_inv, lat_rstd, lat_done, zeroed = (sem(n) for n in ("lat_sq", "lat_inv", "lat_rstd", "lat_done", "zeroed"))
        waits_passed = sem("waits_passed")
        act_turn, dve_turn, pool_turn = (sem(n) for n in ("act_turn", "dve_turn", "pool_turn"))
        cur_done, conv_begun, conv_done, silu_done, sq_done = (sem(n) for n in ("cur_done", "conv_begun", "conv_done", "silu_done", "sq_done"))
        z_done, qn_done, rot_done, qr_done, kn_done, va_done = (sem(n) for n in ("z_done", "qn_done", "rot_done", "qr_done", "kn_done", "va_done"))
        inv16, r16_done, lf_done, src_done, tok_done = (sem(n) for n in ("inv16", "r16_done", "lf_done", "src_done", "tok_done"))
        e_done, arg_done, decay_done, lt_done, qk_done, qd_done = (sem(n) for n in ("e_done", "arg_done", "decay_done", "lt_done", "qk_done", "qd_done"))
        r_done, t_first, t_done, cm_done, x_done = (sem(n) for n in ("r_done", "t_first", "t_done", "cm_done", "x_done"))
        wt_done, u_done, s_done, vnew_done, o_done = (sem(n) for n in ("wt_done", "u_done", "s_done", "vnew_done", "o_done"))
        osq_done, inv8, r8_done, on_done = (sem(n) for n in ("osq_done", "inv8", "r8_done", "on_done"))
        max_done, exp_done, p_done, pt_done = (sem(n) for n in ("max_done", "exp_done", "p_done", "pt_done"))
        m_in = [sem(f"m_in_{b}") for b in range(2)]
        gate_done, merged = sem("gate_done"), sem("merged")
        wo_in, x2_in, row_in, bias_ld, bias_cast, bias_st = (sem(n) for n in ("wo_in", "x2_in", "row_in", "bias_ld", "bias_cast", "bias_st"))
        x2_done, ssx2, inv2, rstd2, h2_done, h2_st, h2T_done = (sem(n) for n in ("x2_done", "ssx2", "inv2", "rstd2", "h2_done", "h2_st", "h2T_done"))
        lgT_done, dif_done, e4_done, msk_done, cnt_done, excl_done, list_src = (sem(n) for n in ("lgT_done", "dif_done", "e4_done", "msk_done", "cnt_done", "excl_done", "list_src"))
        addr_done, table_clear, table_set, tab_in, tok_ready, list_done = (sem(n) for n in ("addr_done", "table_clear", "table_set", "tab_in", "tok_ready", "list_done"))
        chunk_used = sem("chunk_used")
        chunk_in = [sem(f"chunk_in_{c}") for c in range(12)]
        bias_in, ones3_done = sem("bias_in"), sem("ones3_done")
        xg_clear, gix_done, gathered, xt_done, xT_done = (sem(n) for n in ("xg_clear", "gix_done", "gathered", "xt_done", "xT_done"))
        gu_free, g_min, sg_done, act_done = (sem(n) for n in ("gu_free", "g_min", "sg_done", "act_done"))
        at_done, aT_done, ys_done, six_done, scattered, all_rows = (sem(n) for n in ("at_done", "aT_done", "ys_done", "six_done", "scattered", "all_rows"))
        y_in = [sem(f"y_in_{t}") for t in range(NT)]
        last_y_in = [sem(f"last_y_in_{k}") for k in range(1, TOPK)]
        sum_done, ssf, invf, rstdf, out_done, out_st = (sem(n) for n in ("sum_done", "ssf", "invf", "rstdf", "out_done", "out_st"))

        def first(n):
            return isinstance(n, int) and n == 0

        block = ctx.enter_context(nc.Block())

        def w_gu_chunk(e, c):
            half, kk = c // 4, c % 4
            return (w_gu[bass.ds(e, 1), 2 * P * kk:2 * P * (kk + 1), D * half:D * (half + 1)]
                    .rearrange("o (k p) f -> p (o k) f", p=P))

        def w_dn_chunk(e, c):
            kk = c - 8
            return w_dn[bass.ds(e, 1), 2 * P * kk:2 * P * (kk + 1), :].rearrange("o (k p) f -> p (o k) f", p=P)

        @block.sync
        def _(sp):
            for t in range(NT):
                sp.dma_start(xin[:, t, :], x[t * P:(t + 1) * P, :]).then_inc(x_in, 16)
            for dst, src in ((mk[:, :, :], masks), (nw[:, 0:KD], norm_mix), (nw[:, KD:KD + KQ], q_norm),
                             (nw[:, KD + KQ:], kv_norm), (gp[:, 0:8], a_log), (gp[:, 8:16], dt_bias),
                             (dg[:, :], diag), (csn[:, 0, :], cos), (csn[:, 1, :], sin), (gw[:, :], gdn_norm),
                             (cw[:, :, :], conv_w), (sm[:, :], small), (thr[:, :], small[0:32, 96:112]),
                             (wr[:, :, :], w_router), (br[:, :], b_router), (valt[:, :], ints[:, 0:16])):
                sp.dma_start(dst, src).then_inc(const_in, 16)
            sp.dma_start(wba[:, :, :], w_ba).then_inc(w_ba_in, 16)
            sp.dma_start(wcq[:, :, :], w_cq).then_inc(w_cq_in, 16)
            sp.dma_start(wckv[:, :, :], w_ckv).then_inc(w_ckv_in, 16)
            for n in range(4):
                sp.dma_start(wqkvz[n], w_pair[0, n]).then_inc(w_in[n], 16)
            sp.dma_start(wqb, w_qb[0]).then_inc(w_qb_in, 16)
            sp.dma_start(wkb, w_kvb[0]).then_inc(w_kvb_in, 16)
            sp.dma_start(slot_dram.rearrange("(p c) o -> p (c o)", p=P), ints[:, 16:144]).then_inc(table_clear, 16)
            with sp.Fori(0, PAIRS - 1) as i:
                for n, last in enumerate(("q1", "k1", "v1", "z")):
                    sp.wait_ge(filled, PAIR_F.at(last, i))
                    sp.dma_start(wqkvz[n], w_pair[bass.ds(i + 1, 1), n].rearrange("o p k m -> p (o k) m")).then_inc(w_in[n], 16)
                sp.wait_ge(filled, PAIR_F.at("qn", i))
                sp.dma_start(wqb, w_qb[bass.ds(i + 1, 1)].rearrange("o p k m -> p (o k) m")).then_inc(w_qb_in, 16)
                sp.wait_ge(filled, PAIR_F.at("va", i))
                sp.dma_start(wkb, w_kvb[bass.ds(i + 1, 1)].rearrange("o p k m -> p (o k) m")).then_inc(w_kvb_in, 16)
            sp.wait_ge(filled, PAIR_F.at("sc7", PAIRS - 1))
            for b in range(2):
                sp.dma_start(mw[b], w_merge[b]).then_inc(m_in[b], 16)
            sp.wait_ge(act_turn, PAIRS + 1)
            sp.wait_ge(dve_turn, PAIRS + 1)
            for h in range(2):
                sp.dma_start(wo[:, h], w_out[h]).then_inc(wo_in, 16)
            for t in range(NT):
                sp.dma_start(x2[:, t, :], x[t * P:(t + 1) * P, :]).then_inc(x2_in, 16)
            sp.wait_ge(pool_turn, PAIRS + 1)
            sp.dma_start(bfull[:, 0:2 * DE], b_gu).then_inc(bias_ld, 16)
            sp.dma_start(bfull[:, 2 * DE:], b_dn).then_inc(bias_ld, 16)
            with sp.Fori(0, KD // 2 - 1) as i:
                for b in range(2):
                    sp.wait_ge(filled, MERGE_F.at("y0" if b == 0 else "yb1", i))
                    sp.dma_start(mw[b], w_merge[bass.ds(2 * i + (b + 2), 1)]
                                 .rearrange("o p w k m -> p (o w) k m")).then_inc(m_in[b], 16)
            for part in range(3):
                sp.wait_ge(bias_cast, part + 1)
                sp.dma_start(bias_dram[:, part, :], bpart).then_inc(bias_st, 16)
            sp.wait_ge(filled, MERGE_F.at("yb1", KD // 2 - 1))
            sp.dma_start(nrow, norm_ffn.broadcast_to([P, D])).then_inc(row_in, 16)
            sp.wait_ge(merged, KD + 2)

            def expert_weights(n, e, chunks):
                for c in chunks:
                    if not first(n):
                        sp.wait_ge(chunk_used, 12 * n + (c + 1 - 12))
                    src = w_gu_chunk(e, c) if c < 8 else w_dn_chunk(e, c)
                    sp.dma_start(ring[c].rearrange("p (k f) -> p k f", k=2), src).then_inc(chunk_in[c], 16)

            def expert_bias(n, e):
                if not first(n):
                    sp.wait_ge(chunk_used, 12 * n + (9 - 12))
                sp.dma_start(bcur, bias_dram[bass.ds(e, 1)].rearrange("o b f -> (o b) f")).then_inc(bias_in, 16)

            expert_weights(0, 0, range(6))
            sp.wait_ge(bias_st, 48)
            sp.wait_ge(filled, MERGE_F.at("yb1", KD // 2 - 1))
            expert_bias(0, 0)
            sp.wait_ge(filled, OUT_F.at(f"x{NT - 1}"))
            expert_weights(0, 0, range(6, 12))
            for t in range(NT):
                sp.wait_ge(h2_done, t + 1)
                sp.dma_start(h2_dram[t * P:(t + 1) * P, :], h2[:, t, :]).then_inc(h2_st, 16)
            sp.wait_ge(table_set, 16 * NT * TOPK)
            sp.dma_start(tab[:, :], slot_dram.rearrange("(p c) o -> p (c o)", p=P)).then_inc(tab_in, 16)
            with sp.Fori(1, NE) as e:
                expert_weights(e, e, range(9))
                expert_bias(e, e)
                expert_weights(e, e, range(9, 12))
            sp.wait_ge(list_done, 1)
            extra = sp.value_load(lst[0:1, 32:33], min_val=0, max_val=MAX_EXTRA)
            with sp.If(extra > 0):
                with sp.Fori(0, MAX_EXTRA) as j:
                    with sp.If(j < extra):
                        e = sp.value_load(lst[0:1, bass.ds(j + 16, 1)], min_val=0, max_val=NE - 1)
                        expert_weights(j + NE, e, range(9))
                        expert_bias(j + NE, e)
                        expert_weights(j + NE, e, range(9, 12))
            sp.wait_ge(all_rows, 1)
            sp.dma_start(nrow, norm_final.broadcast_to([P, D])).then_inc(row_in, 16)
            for t in range(NT):
                rows_of_tile = y_dram[t * P * TOPK:(t + 1) * P * TOPK, :].rearrange("(p k) d -> p k d", k=TOPK)
                if t < NT - 1:
                    sp.dma_start(yin[t], rows_of_tile).then_inc(y_in[t], 16)
                    continue
                for k in range(TOPK):
                    sp.dma_start(yin[t][:, k, :], rows_of_tile[:, k, :]).then_inc(last_y_in[k - 1] if k else y_in[t], 16)
            for t in range(NT):
                sp.wait_ge(out_done, t + 1)
                sp.dma_start(out[t * P:(t + 1) * P, :], x2[:, t, :]).then_inc(out_st, 16)
            sp.wait_ge(out_st, 16 * NT)

        @block.tensor
        def _(pe):
            def claim(F, name, turn=0):
                n = F.free_before(name, turn)
                if not first(n):
                    pe.wait_ge(region_free[F.region[name]], n)

            def mms(dst, pairs):
                for k, (lhsT, rhs) in enumerate(pairs):
                    ins = pe.matmul(dst, lhsT, rhs, start=(k == 0), stop=(k == len(pairs) - 1))
                return ins

            ident = mk[:, M_ID, :]

            pe.wait_ge(const_in, 16 * 16)
            pe.wait_ge(xn_done, NT)
            for k in range(KD):
                claim(PRE_F, f"h{k}")
                for t in range(NT):
                    ins = pe.transpose(region(PRE_F.region[f"h{k}"], 512)[:, t * P:(t + 1) * P],
                                       xin[:, t, k * P:(k + 1) * P], ident)
                ins.then_inc(filled, 1)
            claim(PRE_F, "ba")
            pe.wait_ge(hT_done, KD)
            pe.wait_ge(w_ba_in, 16)
            for t in range(NT):
                ins = mms(region("A")[:, 16 * t:16 * t + 16],
                          [(hT[:, k, t * P:(t + 1) * P], wba[:, k, :]) for k in range(KD)])
            ins.then_inc(filled, 1)
            pe.wait_ge(w_cq_in, 16)
            for j in range(KQ):
                claim(PRE_F, f"cq{j}")
                mms(region(PRE_F.region[f"cq{j}"], 512),
                    [(wcq[:, k, j * P:(j + 1) * P], hT[:, k, :]) for k in range(KD)]).then_inc(filled, 1)
                if j == 0:
                    claim(PRE_F, "gs")
                    pe.wait_ge(g_done, 1)
                    for n, m in enumerate((M_INCL, M_SAME, M_IND0, M_IND1)):
                        ins = pe.matmul(region("C")[:, 32 * n:32 * n + 32], mk[:, m, :],
                                        gmt[:, 0].rearrange("p t h -> p (t h)"), start=True, stop=True)
                    ins.then_inc(filled, 1)
            pe.wait_ge(w_ckv_in, 16)
            for j, name in enumerate(("kv0", "kv1", "kr")):
                claim(PRE_F, name)
                mms(region(PRE_F.region[name], 512),
                    [(wckv[:, k, j * P:(j + 1) * P], hT[:, k, :]) for k in range(KD)]).then_inc(filled, 1)
            pe.wait_ge(lat_sq, KQ)
            claim(PRE_F, "cqs")
            mms(region("C", 512), [(mk[:, M_ONES, :], csq[:, j, :]) for j in range(KQ)]).then_inc(filled, 1)
            pe.wait_ge(lat_sq, KQ + KKV)
            claim(PRE_F, "kvs")
            mms(region("D", 512), [(mk[:, M_ONES, :], ksq[:, j, :]) for j in range(KKV)]).then_inc(filled, 1)

            with pe.Fori(0, PAIRS) as i:
                F = PAIR_F

                def project(name, n, half):
                    r = two(F.region[name])[:, half, :]
                    mms(r, [(wqkvz[n][:, k, half * P:(half + 1) * P], hT[:, k, :]) for k in range(KD)]).then_inc(filled, 1)

                def squares(j):
                    pe.wait_ge(sq_done, 4 * i + (j + 1))
                    for t in range(NT):
                        ins = pe.matmul(region("D")[:, NT * j + t:NT * j + t + 1], sq[:, j % 2, t * P:(t + 1) * P],
                                        mk[:, M_ONES, 0:1], start=True, stop=True)
                    ins.then_inc(filled, 1)

                def slot(n):
                    if n < UNITS:
                        h, t = n // NT, n % NT
                        claim(F, f"sc{n}", i)
                        if n == 0:
                            pe.wait_ge(qr_done, i + 1)
                            pe.wait_ge(kn_done, i + 1)
                        w = (t + 1) * P
                        mms(region("D")[:, 0:w], [(qn[:, h, t * P:(t + 1) * P], kn[:, h, 0:w]),
                                                  (qr[:, t * P:(t + 1) * P], krp[:, h, 0:w])]).then_inc(filled, 1)
                    if 1 <= n <= UNITS:
                        u = n - 1
                        claim(F, f"pt{u}", i)
                        pe.wait_ge(p_done, UNITS * i + n)
                        for k in range(u % NT + 1):
                            ins = pe.transpose(region("E", 512)[:, k * P:(k + 1) * P], pb[:, u % 2, k * P:(k + 1) * P], ident)
                        ins.then_inc(filled, 1)
                    if 2 <= n:
                        u = n - 2
                        h = u // NT
                        claim(F, f"pv{u}", i)
                        pe.wait_ge(pt_done, UNITS * i + (u + 1))
                        mms(region("E", P), [(va[:, k, h * P:(h + 1) * P], ptb[:, u % 2, k * P:(k + 1) * P])
                                             for k in range(u % NT + 1)]).then_inc(filled, 1)

                pe.wait_ge(w_in[0], 16 * i + 16)
                claim(F, "q0", i)
                project("q0", 0, 0)
                project("q1", 0, 1)
                pe.wait_ge(w_in[1], 16 * i + 16)
                claim(F, "k0", i)
                project("k0", 1, 0)
                claim(F, "ss0", i)
                squares(0)
                project("k1", 1, 1)
                squares(1)
                pe.wait_ge(w_in[2], 16 * i + 16)
                claim(F, "v0", i)
                project("v0", 2, 0)
                squares(2)
                project("v1", 2, 1)
                pe.wait_ge(w_in[3], 16 * i + 16)
                claim(F, "z", i)
                for t in range(NT):
                    ins = mms(region("A")[:, 256 * t:256 * (t + 1)],
                              [(hT[:, k, t * P:(t + 1) * P], wqkvz[3][:, k, :]) for k in range(KD)])
                ins.then_inc(filled, 1)
                squares(3)
                pe.wait_ge(silu_done, 6 * i + 6)
                for name, src in (("kt", kT), ("vt", vT)):
                    claim(F, name, i)
                    for h in range(2):
                        for t in range(NT):
                            ins = pe.transpose(two(F.region[name])[:, h, t * P:(t + 1) * P], src[:, h, t * P:(t + 1) * P], ident)
                    ins.then_inc(filled, 1)
                pe.wait_ge(lat_done, 1)
                pe.wait_ge(zeroed, 2)
                pe.wait_ge(w_qb_in, 16 * i + 16)
                claim(F, "qr", i)
                mms(region("E", 512), [(wqb[:, k, 2 * P:3 * P], cqn[:, k, :]) for k in range(KQ)]).then_inc(filled, 1)
                claim(F, "qn", i)
                for h in range(2):
                    ins = mms(two("A")[:, h, :], [(wqb[:, k, h * P:(h + 1) * P], cqn[:, k, :]) for k in range(KQ)])
                ins.then_inc(filled, 1)
                pe.wait_ge(w_kvb_in, 16 * i + 16)
                claim(F, "kn", i)
                for h in range(2):
                    ins = mms(two("C")[:, h, :], [(wkb[:, k, h * P:(h + 1) * P], kvn[:, k, :]) for k in range(KKV)])
                ins.then_inc(filled, 1)

                def token_rows(n, name, src):
                    claim(F, name, i)
                    pe.wait_ge(src_done, 3 * i + (n + 1))
                    for h in range(2):
                        ins = pe.matmul(two(F.region[name])[:, h, :], mk[:, M_ONES, :],
                                        src[:, NT * h:NT * (h + 1), :].rearrange("p t m -> p (t m)"), start=True, stop=True)
                    ins.then_inc(filled, 1)

                def with_keys(dst, h, src):
                    for t in range(NT):
                        c = slice(t * P, (t + 1) * P)
                        ins = pe.matmul(dst[:, c], kT[:, h, c], src[:, h, c], start=True, stop=True)
                    return ins

                token_rows(0, "rg", sg)
                token_rows(1, "ra", sa)
                for h in range(2):
                    claim(F, f"kk{h}", i)
                    with_keys(region("DE"[h], 512), h, kT).then_inc(filled, 1)
                token_rows(2, "rb", sbq)
                claim(F, "qk", i)
                for h in range(2):
                    ins = with_keys(two("B")[:, h, :], h, qT)
                ins.then_inc(filled, 1)
                claim(F, "va", i)
                for t in range(NT):
                    ins = mms(region("A")[:, 256 * t:256 * (t + 1)],
                              [(kvn[:, k, t * P:(t + 1) * P], wkb[:, k, 2 * P:4 * P]) for k in range(KKV)])
                ins.then_inc(filled, 1)
                pe.wait_ge(r_done, len(LEVELS) * i + 1)
                for h in range(2):
                    claim(F, f"t1_{h}", i)
                    for t in range(NT):
                        ins = pe.transpose(region("DE"[h], 512)[:, t * P:(t + 1) * P], R[:, NT * h + t, :], ident)
                    ins.then_inc(filled, 1)

                def eight(name, lhs, rhs):
                    for u in range(2 * NT):
                        ins = pe.matmul(region(F.region[name])[:, u * P:(u + 1) * P], lhs[:, u, :], rhs[:, u, :],
                                        start=True, stop=True)
                    ins.then_inc(filled, 1)

                for n, s in enumerate(LEVELS[1:]):
                    claim(F, f"x{s}", i)
                    pe.wait_ge(cm_done, (len(LEVELS) - 1) * i + (n + 1))
                    if n == 0:
                        pe.wait_ge(t_first, i + 1)
                    else:
                        pe.wait_ge(t_done, (len(LEVELS) - 2) * i + n)
                    eight(f"x{s}", cm, T)
                    slot(n)
                    pe.wait_ge(x_done, (len(LEVELS) - 1) * i + (n + 1))
                    pe.wait_ge(r_done, len(LEVELS) * i + (n + 1))
                    if s != LEVELS[-1]:
                        claim(F, f"tx{s}", i)
                        eight(f"tx{s}", R, X)
                    claim(F, f"tr{s}", i)
                    eight(f"tr{s}", X, R)
                pe.wait_ge(r_done, len(LEVELS) * i + len(LEVELS))
                pe.wait_ge(tok_done, 3 * i + 3)
                claim(F, "wt", i)
                eight("wt", kbg, R)
                claim(F, "u", i)
                eight("u", R, vb)
                pe.wait_ge(wt_done, i + 1)
                pe.wait_ge(qd_done, i + 1)
                pe.wait_ge(qk_done, i + 1)
                for c in range(NC):
                    t, par = c // 2, c % 2
                    claim(F, f"ws{c}", i)
                    pe.wait_ge(s_done, (NC + 1) * i + (c + 1))
                    for h in range(2):
                        ins = pe.matmul(two("A")[:, 0, h * P:(h + 1) * P], WT[:, NT * h + t, :], state[:, c % 2, h, :],
                                        start=True, stop=True)
                    ins.then_inc(filled, 1)
                    if c < SCAN_SLOTS:
                        slot(len(LEVELS) - 1 + c)
                    pe.wait_ge(vnew_done, NC * i + (c + 1))
                    for h in range(2):
                        ins = pe.matmul(two("A")[:, 1, h * P:(h + 1) * P], kd[:, NT * h + t, :], vnew[:, par, h, :],
                                        start=True, stop=True)
                    ins.then_inc(filled, 1)
                    claim(F, f"o{c}", i)
                    for h in range(2):
                        ins = mms(two("BC"[par])[:, h, 0:P],
                                  [(qT[:, h, t * P:(t + 1) * P], state[:, c % 2, h, :]),
                                   (qk[:, NT * h + t, :], vnew[:, par, h, :])])
                    ins.then_inc(filled, 1)
                pe.wait_ge(on_done, NT * i + NT)
                for h in range(2):
                    claim(F, f"ot{h}", i)
                    for t in range(NT):
                        ins = pe.transpose(region("DE"[h], 512)[:, t * P:(t + 1) * P], osb[:, t, h, :], ident)
                    ins.then_inc(filled, 1)

            pe.wait_ge(act_turn, PAIRS + 1)
            with pe.Fori(0, KD // 2) as i:
                F = MERGE_F
                for b in range(2):
                    claim(F, f"g{b}", i)
                    pe.wait_ge(m_in[b], 16 * i + 16)
                    for n in range(2):
                        ins = mms(two(F.region[f"g{b}"])[:, n, :], [(mw[b][:, n, k, :], hT[:, k, :]) for k in range(KD)])
                    ins.then_inc(filled, 1)
                    for n, src in enumerate((oaT, obT)):
                        name = "y0" if b == 0 else ("ya1", "yb1")[n]
                        if b == 1 or n == 0:
                            claim(F, name, i)
                        dst = two("B")[:, n, :] if b == 0 else region("DE"[n], 512)
                        ins = mms(dst, [(mw[b][:, 2 + n, k, :], src[:, k, :]) for k in range(KD)])
                        if b == 1 or n == 1:
                            ins.then_inc(filled, 1)

            F = OUT_F
            pe.wait_ge(merged, KD + 2)
            pe.wait_ge(wo_in, 32)
            for t in range(NT):
                claim(F, f"x{t}")
                for h in range(2):
                    ins = mms(two(F.region[f"x{t}"])[:, h, :], [(mT[:, k, t * P:(t + 1) * P], wo[:, h, k, :]) for k in range(KD)])
                ins.then_inc(filled, 1)
            pe.wait_ge(h2_done, NT)
            for k in range(KD):
                claim(F, f"r{k}")
                for t in range(NT):
                    ins = pe.transpose(region(F.region[f"r{k}"], 512)[:, t * P:(t + 1) * P], h2[:, t, k * P:(k + 1) * P], ident)
                ins.then_inc(filled, 1)
            claim(F, "lg")
            pe.wait_ge(h2T_done, KD)
            mms(region("A", 512)[0:NE, :], [(wr[:, k, :], h2T[:, k, :]) for k in range(KD)]).then_inc(filled, 1)
            claim(F, "lt")
            pe.wait_ge(lgT_done, 1)
            for t in range(NT):
                ins = pe.transpose(region("B")[:, NE * t:NE * (t + 1)], lgT[:, t * P:(t + 1) * P], mk[0:NE, M_ID, 0:NE])
            ins.then_inc(filled, 1)
            claim(F, "pos")
            pe.wait_ge(msk_done, 1)
            for t in range(NT):
                ins = mms(region("C")[:, NE * t:NE * (t + 1)],
                          [(mk[:, M_ONES, :], msk[:, u, :]) for u in range(t)] + [(mk[:, M_BEFORE, :], msk[:, t, :])])
            ins.then_inc(filled, 1)
            claim(F, "tot")
            mms(region("D")[0:NE, 0:1], [(msk[:, t, :], mk[:, M_ONES, 0:1]) for t in range(NT)]).then_inc(filled, 1)
            claim(F, "ex")
            pe.wait_ge(cnt_done, 1)
            pe.matmul(region("E", 512)[0:NE, 0:1], mk[0:NE, M_BEFORE, 0:NE], tot[:, 0:1], start=True, stop=True).then_inc(filled, 1)
            claim(F, "li")
            pe.wait_ge(list_src, 1)
            pe.matmul(region("A")[0:1, 0:97], mk[0:NE, M_ONES, 0:1], ol, start=True, stop=True).then_inc(filled, 1)

            pe.wait_ge(list_done, 1)

            def token_columns(n):
                pe.wait_ge(gathered, 16 * n + 16)
                if not first(n):
                    pe.wait_ge(aT_done, 2 * n)
                for k in range(KD):
                    ins = pe.transpose(region("C")[:, k * P:(k + 1) * P], xg[:, k * P:(k + 1) * P], ident)
                ins.then_inc(xt_done, 1)

            def bias_rows(dst, col):
                for h in range(2):
                    pe.matmul(dst[:, h, :], ones3[:, :], bcur[:, col + 512 * h:col + 512 * (h + 1)], start=True, stop=False)

            def up(n, half, kk):
                c = 4 * half + kk
                pe.wait_ge(chunk_in[c], 16 * n + 16)
                w = ring[c].rearrange("p (k f) -> p k f", k=2)
                for k in range(2):
                    for h in range(2):
                        ins = pe.matmul(two("AB"[half])[:, h, :], xT[:, 2 * kk + k, :], w[:, k, 512 * h:512 * (h + 1)],
                                        start=False, stop=(kk == 3 and k == 1))
                ins.then_inc(chunk_used, 1)
                return ins

            def down(n, kk):
                c = 8 + kk
                pe.wait_ge(chunk_in[c], 16 * n + 16)
                w = ring[c].rearrange("p (k f) -> p k f", k=2)
                for k in range(2):
                    for h in range(2):
                        ins = pe.matmul(yd[:, h, :], aT[:, 2 * kk + k, :], w[:, k, 512 * h:512 * (h + 1)],
                                        start=False, stop=(kk == 3 and k == 1))
                ins.then_inc(chunk_used, 1)

            def act_columns(n, half):
                pe.wait_ge(act_done, 2 * n + (half + 1))
                for k in range(4):
                    ins = pe.transpose(two("C")[:, half, k * P:(k + 1) * P], act[:, half, k * P:(k + 1) * P], ident)
                ins.then_inc(at_done, 1)

            def expert(n, next_block):
                pe.wait_ge(bias_in, 16 * n + 16)
                if not first(n):
                    pe.wait_ge(gu_free, 2 * n)
                pe.wait_ge(xT_done, n + 1)
                bias_rows(two("A"), 0)
                for kk in range(4):
                    up(n, 0, kk)
                bias_rows(two("B"), DE)
                for kk in range(3):
                    up(n, 1, kk)
                act_columns(n, 0)
                up(n, 1, 3)
                if not first(n):
                    pe.wait_ge(ys_done, n)
                bias_rows(yd, 2 * DE)
                pe.wait_ge(aT_done, 2 * n + 1)
                down(n, 0)
                act_columns(n, 1)
                down(n, 1)
                pe.wait_ge(aT_done, 2 * n + 2)
                down(n, 2)
                if next_block:
                    token_columns(n + 1)
                down(n, 3)

            pe.wait_ge(ones3_done, 1)
            token_columns(0)
            expert(0, True)
            with pe.Fori(1, NE - 1) as n:
                expert(n, True)
            expert(NE - 1, False)
            extra = pe.value_load(lst[0:1, 32:33], min_val=0, max_val=MAX_EXTRA)
            with pe.If(extra > 0):
                with pe.Fori(0, MAX_EXTRA) as j:
                    with pe.If(j < extra):
                        token_columns(j + NE)
                        expert(j + NE, False)

        @block.scalar
        def _(act_e):
            ac = act_e

            def copy(dst, src, scale=None):
                if scale is None:
                    return ac.activation(dst, src, ACT.Copy)
                return ac.activation(dst, src, ACT.Copy, scale=scale)

            def swap_halves(src):
                for p in (0, 64):
                    copy(rot[p:p + 32, :], src[p + 32:p + 64, :])
                    ins = copy(rot[p + 32:p + 64, :], src[p:p + 32, :])
                return ins

            ac.wait_ge(x_in, 16 * NT)
            for t in range(NT):
                ins = ac.activation(csq[:, 2 * (t % 2):2 * (t % 2) + 2, :].rearrange("p a s -> p (a s)"), xin[:, t, :],
                                    ACT.Square, accum_out=r4[:, 0, t:t + 1])
                ac.drain()
            ac.drain().then_inc(ssx_done, 1)
            ac.wait_ge(ssx_done, 2)
            ac.activation(r4[:, 1, :], r4[:, 1, :], ACT.Sqrt).then_inc(rstd_done, 1)
            ac.wait_ge(const_in, 16 * 16)
            for k in range(KD):
                ac.wait_ge(filled, PRE_F.at(f"h{k}"))
                copy(hT[:, k, :], region(PRE_F.region[f"h{k}"], 512), nw[:, k:k + 1]).then_inc(region_free[PRE_F.region[f"h{k}"]], 1)
            ac.drain().then_inc(hT_done, KD)
            ac.wait_ge(pre_step, 1)
            ac.activation(gmt[:, 1], gmt[:, 1], ACT.Sigmoid)
            ac.activation(gp[:, 0:8], gp[:, 0:8], ACT.Exp)
            ac.drain().then_inc(pre_act, 1)
            ac.activation(gmt[:, 3], gmt[:, 3], ACT.Exp).then_inc(pre_act, 1)
            ac.wait_ge(pre_step, 2)
            ac.activation(gmt[:, 3], gmt[:, 3], ACT.Ln).then_inc(pre_act, 1)
            ac.wait_ge(pre_step, 3)
            for n in (2, 3, 4, 5):
                ac.activation(gmt[:, n], gmt[:, n], ACT.Exp)
            ac.drain().then_inc(pre_act, 1)
            for j in range(KQ + KKV):
                ac.wait_ge(lat_raw, j + 1)
                ac.activation(csq[:, j, :] if j < KQ else ksq[:, j - KQ, :], cqn[:, j, :] if j < KQ else kvn[:, j - KQ, :],
                              ACT.Square).then_inc(lat_sq, 1)
            ac.wait_ge(filled, PRE_F.at("kr"))
            swap_halves(region("B", 512)).then_inc(region_free["B"], 1)
            ac.drain().then_inc(rot_done, 1)
            ac.wait_ge(lat_inv, 1)
            ac.activation(inv[:, :, :], inv[:, :, :], ACT.Sqrt).then_inc(lat_rstd, 1)
            ac.wait_ge(lat_done, 1)
            ac.sem_inc(act_turn, 1)

            with ac.Fori(0, PAIRS) as i:
                F = PAIR_F
                ac.wait_ge(dve_turn, i + 1)
                ac.wait_ge(pool_turn, i + 1)
                ac.wait_ge(cur_done, i + 1)

                def silu(j):
                    ac.wait_ge(conv_done, 6 * i + (j + 1))
                    ac.activation(qkvT[:, j, :], cv[:, j % 2, :], ACT.Silu).then_inc(silu_done, 1)
                    if j < 4:
                        ac.wait_ge(silu_done, 6 * i + (j + 1))
                        if j >= 2:
                            ac.wait_ge(filled, F.at(f"ss{j - 2}", i))
                        ac.activation(sq[:, j % 2, :], qkvT[:, j, :], ACT.Square).then_inc(sq_done, 1)

                for j, name in enumerate(("q0", "q1", "k0", "k1", "v0", "v1")):
                    ac.wait_ge(filled, F.at(name, i))
                    copy(cv[:, j % 2, :], two(F.region[name])[:, j % 2, :], taps[:, j, 3:4]).then_inc(conv_begun, 1)
                    if j >= 1:
                        silu(j - 1)
                silu(5)
                ac.wait_ge(filled, F.at("z", i))
                ac.activation(zs, region("A").rearrange("p (t c) -> p t c", t=NT), ACT.Silu).then_inc(region_free["A"], 1)
                ac.drain().then_inc(z_done, 1)
                ac.wait_ge(inv16, i + 1)
                ac.activation(r16[:, :], r16[:, :], ACT.Sqrt).then_inc(r16_done, 1)
                ac.wait_ge(filled, F.at("qr", i))
                swap_halves(region("E", 512)).then_inc(region_free["E"], 1)
                ac.drain().then_inc(rot_done, 1)
                ac.wait_ge(filled, F.at("qn", i))
                copy(qn, two("A")).then_inc(region_free["A"], 1)
                ac.wait_ge(filled, F.at("kn", i))
                copy(kn, two("C")).then_inc(region_free["C"], 1)
                ac.wait_ge(filled, F.at("rg", i))
                ac.activation(er, region("B").rearrange("p (u m) -> p u m", m=P), ACT.Exp).then_inc(e_done, 1)
                ac.drain().then_inc(region_free["B"], 1)
                ac.wait_ge(arg_done, i + 1)
                ac.activation(dt_, dt_, ACT.Exp).then_inc(decay_done, 1)
                ac.wait_ge(filled, F.at("va", i))
                copy(va, region("A").rearrange("p (t c) -> p t c", t=NT)).then_inc(region_free["A"], 1)
                ac.drain().then_inc(kn_done, 1)
                for h in range(2):
                    ac.wait_ge(filled, F.at(f"t1_{h}", i))
                    copy(T[:, NT * h:NT * (h + 1), :], region("DE"[h], 512).rearrange("p (u m) -> p u m", m=P)).then_inc(region_free["DE"[h]], 1)
                ac.drain().then_inc(t_first, 1)

                def slot(n):
                    if 1 <= n <= UNITS:
                        u = n - 1
                        w = (u % NT + 1) * P
                        ac.wait_ge(filled, F.at(f"pt{u}", i))
                        copy(ptb[:, u % 2, 0:w], region("E", 512)[:, 0:w]).then_inc(pt_done, 1)
                        ac.drain().then_inc(region_free["E"], 1)
                    if 2 <= n:
                        u = n - 2
                        h, t = u // NT, u % NT
                        ac.wait_ge(filled, F.at(f"pv{u}", i))
                        copy(obT[:, bass.ds(2 * i + h, 1), t * P:(t + 1) * P].rearrange("p o s -> p (o s)"),
                             region("E", P)).then_inc(region_free["E"], 1)
                    if n < UNITS:
                        w = (n % NT + 1) * P
                        ac.wait_ge(max_done, UNITS * i + (n + 1))
                        ac.activation(pb[:, n % 2, 0:w], region("D")[:, 0:w], ACT.Exp, bias=nm[:, 1, n:n + 1], scale=ATT_SCALE,
                                      accum_out=nm[:, 2, n:n + 1]).then_inc(region_free["D"], 1)
                        ac.drain().then_inc(exp_done, 1)

                for n, s in enumerate(LEVELS[1:]):
                    ac.wait_ge(filled, F.at(f"x{s}", i))
                    copy(X, region("A").rearrange("p (u m) -> p u m", m=P)).then_inc(x_done, 1)
                    ac.drain().then_inc(region_free["A"], 1)
                    slot(n)
                ac.wait_ge(filled, F.at("wt", i))
                copy(WT, region("A").rearrange("p (u m) -> p u m", m=P)).then_inc(region_free["A"], 1)
                ac.wait_ge(filled, F.at("u", i))
                copy(U, region("B").rearrange("p (u m) -> p u m", m=P)).then_inc(region_free["B"], 1)
                ac.drain().then_inc(wt_done, 1)

                def rstd_of_rows(t):
                    ac.wait_ge(inv8, NT * i + (t + 1))
                    ac.activation(r8[:, 2 * t:2 * t + 2], r8[:, 2 * t:2 * t + 2], ACT.Sqrt).then_inc(r8_done, 1)

                for c in range(NC):
                    if c < SCAN_SLOTS:
                        slot(len(LEVELS) - 1 + c)
                    t, par = c // 2, c % 2
                    rows = slice(CHUNK * par, CHUNK * (par + 1))
                    ac.wait_ge(filled, F.at(f"o{c}", i))
                    copy(osb[rows, t], two("BC"[par])[rows, :, 0:P]).then_inc(region_free["BC"[par]], 1)
                    if par == 1:
                        ac.drain().then_inc(o_done, 1)
                        ac.wait_ge(o_done, NT * i + (t + 1))
                        for h in range(2):
                            ac.activation(cm[:, h, :], osb[:, t, h, :], ACT.Square, accum_out=r8[:, 2 * t + h:2 * t + h + 1])
                        ac.drain().then_inc(osq_done, 1)
                    elif t >= 1:
                        rstd_of_rows(t - 1)
                rstd_of_rows(NT - 1)
                for h in range(2):
                    ac.wait_ge(filled, F.at(f"ot{h}", i))
                    copy(oaT[:, bass.ds(2 * i + h, 1), :].rearrange("p o s -> p (o s)"), region("DE"[h], 512)).then_inc(region_free["DE"[h]], 1)
                ac.drain().then_inc(act_turn, 1)

            with ac.Fori(0, KD // 2) as i:
                for b in range(2):
                    r = MERGE_F.region[f"g{b}"]
                    ac.wait_ge(filled, MERGE_F.at(f"g{b}", i))
                    ac.wait_ge(merged, 2 * i + 2)
                    ac.activation(gs_[b], two(r), ACT.Sigmoid).then_inc(region_free[r], 1)
                    ac.drain().then_inc(gate_done, 1)

            F = OUT_F
            for t in range(NT):
                ac.wait_ge(x2_done, t + 1)
                ac.activation(junk, x2[:, t, :], ACT.Square, accum_out=r4[:, 0, t:t + 1])
                ac.drain()
            ac.drain().then_inc(ssx2, 1)
            ac.wait_ge(inv2, 1)
            ac.activation(r4[:, 1, :], r4[:, 1, :], ACT.Sqrt).then_inc(rstd2, 1)
            for k in range(KD):
                r = F.region[f"r{k}"]
                ac.wait_ge(filled, F.at(f"r{k}"))
                copy(h2T[:, k, :], region(r, 512)).then_inc(region_free[r], 1)
            ac.drain().then_inc(h2T_done, KD)
            ac.wait_ge(filled, F.at("lg"))
            copy(lgT, region("A", 512)[0:NE, :]).then_inc(region_free["A"], 1)
            ac.drain().then_inc(lgT_done, 1)
            ac.wait_ge(dif_done, 1)
            ac.activation(e4, e4, ACT.Exp).then_inc(e4_done, 1)

            def columns(n):
                ac.wait_ge(xt_done, n + 1)
                copy(xT, region("C").rearrange("p (k m) -> p k m", k=KD)).then_inc(xT_done, 1)

            def expert(n, next_block):
                for half in range(2):
                    ac.wait_ge(g_min, 2 * n + (half + 1))
                    ac.activation(sgm, gb, ACT.Sigmoid, scale=ALPHA).then_inc(sg_done, 1)
                    ac.wait_ge(at_done, 2 * n + (half + 1))
                    copy(aT[:, 4 * half:4 * half + 4, :], two("C")[:, half, :].rearrange("p (k m) -> p k m", k=4)).then_inc(aT_done, 1)
                if next_block:
                    columns(n + 1)
                ac.wait_ge(chunk_used, 12 * n + 12)
                if not first(n):
                    ac.wait_ge(scattered, 16 * n)
                copy(ys, yd.rearrange("p h s -> p (h s)")).then_inc(ys_done, 1)

            ac.wait_ge(list_done, 1)
            columns(0)
            expert(0, True)
            with ac.Fori(1, NE - 1) as n:
                expert(n, True)
            expert(NE - 1, False)
            extra = ac.value_load(lst[0:1, 32:33], min_val=0, max_val=MAX_EXTRA)
            with ac.If(extra > 0):
                with ac.Fori(0, MAX_EXTRA) as j:
                    with ac.If(j < extra):
                        columns(j + NE)
                        expert(j + NE, False)

            for t in range(NT):
                ac.wait_ge(sum_done, t + 1)
                ac.activation(junk, x2[:, t, :], ACT.Square, accum_out=r4[:, 0, t:t + 1])
                ac.drain().then_inc(ssf, 1)
                ac.wait_ge(invf, t + 1)
                ac.activation(r4[:, 1, t:t + 1], r4[:, 1, t:t + 1], ACT.Sqrt).then_inc(rstdf, 1)

        @block.vector
        def _(dv):
            def tt(o, a, b, op=ALU.mult):
                return dv.tensor_tensor(o, a, b, op)

            def stt(o, a, s, b, op0=ALU.mult, op1=ALU.mult):
                return dv.scalar_tensor_tensor(out=o, in0=a, scalar=s, in1=b, op0=op0, op1=op1)

            def over(v):
                return v.rearrange("p h t -> p (h t)").unsqueeze(2).broadcast_to([P, 2 * NT, P])

            def reg8(r):
                return region(r).rearrange("p (u m) -> p u m", m=P)

            def inverse_mean(dst, src, n, eps=EPS):
                dv.tensor_scalar(dst, src, 1.0 / n, eps, ALU.mult, ALU.add)
                dv.drain()
                return dv.reciprocal(dst, dst)

            m_of = lambda m: mk[:, m, :].unsqueeze(1).broadcast_to([P, 2 * NT, P])

            dv.wait_ge(ssx_done, 1)
            inverse_mean(r4[:, 1, :], r4[:, 0, :], D).then_inc(ssx_done, 1)
            dv.wait_ge(rstd_done, 1)
            for t in range(NT):
                dv.tensor_scalar(xin[:, t, :], xin[:, t, :], r4[:, 1, t:t + 1], None, ALU.mult).then_inc(xn_done, 1)
            dv.wait_ge(const_in, 16 * 16)
            dv.wait_ge(filled, PRE_F.at("ba"))
            ba = region("A")[:, 0:64].rearrange("p (t c) -> p t c", t=NT)
            dv.tensor_copy(gmt[:, 1], ba[:, :, 0:8])
            tt(gmt[:, 2], ba[:, :, 8:16], gp[:, 8:16].unsqueeze(1).broadcast_to([P, NT, HEADS]), ALU.add).then_inc(region_free["A"], 1)
            dv.drain()
            stt(gmt[:, 3], gmt[:, 2], -1.0, gmt[:, 2], ALU.mult, ALU.min).then_inc(pre_step, 1)
            dv.wait_ge(pre_act, 2)
            dv.tensor_scalar(gmt[:, 3], gmt[:, 3], 1.0, None, ALU.add).then_inc(pre_step, 1)
            dv.wait_ge(pre_act, 3)
            stt(gmt[:, 2], gmt[:, 2], 0.0, gmt[:, 3], ALU.max, ALU.add)
            dv.drain()
            stt(gmt[:, 0], gmt[:, 2], -1.0, gp[:, 0:8].unsqueeze(1).broadcast_to([P, NT, HEADS]))
            dv.drain().then_inc(g_done, 1)
            dv.wait_ge(filled, PRE_F.at("gs"))
            sums = region("C")[:, 0:128].rearrange("p (n t h) -> p n t h", n=4, t=NT)

            def factor(n):
                return fac[:, :, n, :].rearrange("p h t -> p t h")

            dv.tensor_copy(factor(F_G), gmt[:, 0])
            dv.tensor_copy(factor(F_BETA), gmt[:, 1])
            dv.tensor_copy(factor(F_GC), sums[:, 0])
            dv.tensor_copy(gmt[:, 2], sums[:, 0])
            dv.tensor_copy(gmt[:, 4:6], sums[:, 2:4])
            dv.drain()
            tt(gmt[:, 3], sums[:, 1], gmt[:, 2], ALU.subtract).then_inc(region_free["C"], 1)
            dv.drain().then_inc(pre_step, 1)
            dv.wait_ge(pre_act, 4)
            tt(factor(F_BEG), gmt[:, 1], gmt[:, 2])
            dv.tensor_copy(factor(F_EKD), gmt[:, 3])
            dv.tensor_copy(factor(F_GL0), gmt[:, 4])
            dv.tensor_copy(factor(F_GL1), gmt[:, 5])
            dv.drain()
            lat = [(f"cq{j}", cqn[:, j, :]) for j in range(KQ)] + [(f"kv{j}", kvn[:, j, :]) for j in range(KKV)]
            for name, dst in lat:
                dv.wait_ge(filled, PRE_F.at(name))
                dv.tensor_copy(dst, region(PRE_F.region[name], 512)).then_inc(region_free[PRE_F.region[name]], 1)
                dv.drain().then_inc(lat_raw, 1)

            def rotate(src, cos_tmp, free):
                tt(cos_tmp, src, csn[:, 0, :]).then_inc(region_free[free], 1)
                tt(rot, rot, csn[:, 1, :])
                dv.drain()

            dv.wait_ge(rot_done, 1)
            rotate(region("B", 512), qr, "B")
            dv.wait_ge(zeroed, 2)
            for h, p in enumerate((slice(0, 64), slice(64, 128))):
                tt(krp[p, h, :], qr[p, :], rot[p, :], ALU.add)
            for n, (name, width) in enumerate((("cqs", Q_LORA), ("kvs", KV_LORA))):
                dv.wait_ge(filled, PRE_F.at(name))
                r = PRE_F.region[name]
                dv.tensor_scalar(inv[:, n, :], region(r, 512), 1.0 / width, EPS, ALU.mult, ALU.add).then_inc(region_free[r], 1)
                dv.drain()
                dv.reciprocal(inv[:, n, :], inv[:, n, :])
            dv.drain().then_inc(lat_inv, 1)
            dv.wait_ge(lat_rstd, 1)
            for j, (name, dst) in enumerate(lat):
                stt(dst, dst, nw[:, KD + j:KD + j + 1], inv[:, 0 if j < KQ else 1, :])
            dv.drain().then_inc(lat_done, 1)
            dv.sem_inc(dve_turn, 1)

            with dv.Fori(0, PAIRS) as i:
                F = PAIR_F
                dv.wait_ge(act_turn, i + 1)
                dv.wait_ge(pool_turn, i + 1)
                dv.tensor_copy(taps.rearrange("p a b -> p (a b)"), cw[:, bass.ds(i, 1), :].rearrange("p o c -> p (o c)"))
                dv.tensor_copy(fcur[:, :, :, :].rearrange("p h f t -> p h (f t)"),
                               fac[:, bass.ds(2 * i, 2), :, :].rearrange("p h f t -> p h (f t)"))
                dv.memset(state[:, 0], 0.0).then_inc(s_done, 1)
                dv.drain().then_inc(cur_done, 1)
                for j, name in enumerate(("q0", "q1", "k0", "k1", "v0", "v1")):
                    dv.wait_ge(conv_begun, 6 * i + (j + 1))
                    r = F.region[name]
                    src, acc = two(r)[:, j % 2, :], cv[:, j % 2, :]
                    for back in (1, 2, 3):
                        ins = stt(acc[:, back:], src[:, 0:SEQ - back], taps[:, j, 3 - back:4 - back], acc[:, back:], ALU.mult, ALU.add)
                        if back < 3:
                            dv.drain()
                    ins.then_inc(region_free[r], 1)
                    dv.drain().then_inc(conv_done, 1)
                dv.wait_ge(filled, F.at("ss3", i))
                dv.tensor_scalar(r16[:, :], region("D")[:, 0:16], EPS, None, ALU.add).then_inc(region_free["D"], 1)
                dv.drain()
                dv.reciprocal(r16[:, :], r16[:, :]).then_inc(inv16, 1)
                dv.wait_ge(r16_done, i + 1)
                rq, rk_ = (r16[:, 8 * n:8 * n + 8].rearrange("p (h t) -> p h t", h=2) for n in range(2))
                tt(lf[:, 0], fcur[:, :, F_BEG, :], rk_)
                tt(lf[:, 1], fcur[:, :, F_EKD, :], rk_)
                tt(lf[:, 2], fcur[:, :, F_BETA, :], rk_)
                dv.tensor_scalar(lf[:, 3], rq, GDN_SCALE, None, ALU.mult)
                dv.drain().then_inc(lf_done, 1)
                dv.wait_ge(filled, F.at("kt", i))
                tt(kbg, reg8("B"), over(lf[:, 0])).then_inc(tok_done, 1)
                tt(kd, reg8("B"), over(lf[:, 1])).then_inc(tok_done, 1)
                dv.drain().then_inc(region_free["B"], 1)
                dv.wait_ge(filled, F.at("vt", i))
                beta = fcur[:, :, F_BETA, :]
                for h in range(2):
                    ins = tt(vb[:, NT * h:NT * (h + 1), :], reg8("C")[:, NT * h:NT * (h + 1), :],
                             beta[:, h, :].unsqueeze(2).broadcast_to([P, NT, P]))
                ins.then_inc(tok_done, 1)
                dv.drain().then_inc(region_free["C"], 1)
                dv.wait_ge(rot_done, i + 2)
                rotate(region("E", 512), qr, "E")
                tt(qr, qr, rot, ALU.add).then_inc(qr_done, 1)
                dv.wait_ge(z_done, i + 1)
                z8 = zs.rearrange("p t (h d) -> p (t h) d", h=2)
                tt(z8, z8, gw[:, :].unsqueeze(1).broadcast_to([P, 2 * NT, P]))
                dv.wait_ge(e_done, i + 1)
                for h in range(2):
                    ins = tt(dt_[:, NT * h:NT * (h + 1), :], reg8("B")[:, NT * h:NT * (h + 1), :],
                             fcur[:, h, F_GC, :].unsqueeze(2).broadcast_to([P, NT, P]), ALU.subtract)
                ins.then_inc(region_free["B"], 1)
                dv.drain()
                dv.tensor_scalar(dt_, dt_, 0.0, None, ALU.min).then_inc(arg_done, 1)
                dv.wait_ge(decay_done, i + 1)
                tt(dt_, dt_, over(rk_))
                dv.drain()
                dv.wait_ge(filled, F.at("ra", i))
                tt(lt_, dt_, reg8("A")).then_inc(region_free["A"], 1)
                dv.drain()
                for h in range(2):
                    dv.wait_ge(filled, F.at(f"kk{h}", i))
                    tt(lt_[:, NT * h:NT * (h + 1), :], lt_[:, NT * h:NT * (h + 1), :],
                       region("DE"[h], 512).rearrange("p (t m) -> p t m", m=P)).then_inc(region_free["DE"[h]], 1)
                dv.drain().then_inc(lt_done, 1)
                dv.wait_ge(filled, F.at("rb", i))
                tt(X, lt_, m_of(M_LEVEL))
                dv.drain()
                stt(R, X, -1.0, m_of(M_ID), ALU.mult, ALU.add).then_inc(r_done, 1)
                tt(qk, dt_, m_of(M_INCL))
                tt(er, er, reg8("C"))
                dv.drain()
                tt(qk, qk, reg8("C")).then_inc(region_free["C"], 1)
                dv.drain()
                dv.wait_ge(filled, F.at("qk", i))
                tt(qT.rearrange("p h (t m) -> p (h t) m", m=P), qT.rearrange("p h (t m) -> p (h t) m", m=P), er).then_inc(qd_done, 1)
                tt(qk, qk, reg8("B")).then_inc(region_free["B"], 1)
                dv.drain().then_inc(qk_done, 1)

                def slot_max(n):
                    if n < UNITS:
                        t = n % NT
                        w = (t + 1) * P
                        s = region("D")
                        dv.wait_ge(filled, F.at(f"sc{n}", i))
                        tt(s[:, w - P:w], s[:, w - P:w], dg[:, :], ALU.add)
                        dv.drain()
                        dv.tensor_reduce(nm[:, 0, n:n + 1], s[:, 0:w], AXX, ALU.max)
                        dv.drain()
                        dv.tensor_scalar(nm[:, 1, n:n + 1], nm[:, 0, n:n + 1], -ATT_SCALE, None, ALU.mult).then_inc(max_done, 1)

                def slot_scale(n):
                    if n < UNITS:
                        w = (n % NT + 1) * P
                        dv.wait_ge(exp_done, UNITS * i + (n + 1))
                        dv.reciprocal(nm[:, 0, n:n + 1], nm[:, 2, n:n + 1])
                        dv.drain()
                        dv.tensor_scalar(pb[:, n % 2, 0:w], pb[:, n % 2, 0:w], nm[:, 0, n:n + 1], None, ALU.mult).then_inc(p_done, 1)

                for n, s in enumerate(LEVELS[1:]):
                    slot_max(n)
                    if s != LEVELS[-1]:
                        dv.wait_ge(filled, F.at(f"tx{s}", i))
                        tt(T, T, reg8("B"), ALU.subtract).then_inc(region_free["B"], 1)
                        dv.drain().then_inc(t_done, 1)
                    dv.wait_ge(filled, F.at(f"tr{s}", i))
                    tt(R, R, reg8("C"), ALU.subtract).then_inc(region_free["C"], 1)
                    dv.drain().then_inc(r_done, 1)
                    slot_scale(n)
                def inverse_of_rows(t):
                    r = r8[:, 2 * t:2 * t + 2]
                    dv.wait_ge(osq_done, NT * i + (t + 1))
                    inverse_mean(r, r, P).then_inc(inv8, 1)

                def outputs_norm(t):
                    dv.wait_ge(r8_done, NT * i + (t + 1))
                    for h in range(2):
                        ins = stt(osb[:, t, h, :], osb[:, t, h, :], r8[:, 2 * t + h:2 * t + h + 1], zs[:, t, h * P:(h + 1) * P])
                    ins.then_inc(on_done, 1)

                dv.wait_ge(wt_done, i + 1)
                for c in range(NC):
                    t, par = c // 2, c % 2
                    rows = slice(CHUNK * par, CHUNK * (par + 1))
                    u_rows = U.rearrange("p (h t) m -> p t h m", h=2)[rows, t]
                    if c < SCAN_SLOTS:
                        slot_max(len(LEVELS) - 1 + c)
                    dv.wait_ge(filled, F.at(f"ws{c}", i))
                    tt(vnew[rows, par], u_rows, two("A")[rows, 0, 0:256].rearrange("p (h d) -> p h d", h=2), ALU.subtract).then_inc(vnew_done, 1)
                    dv.wait_ge(filled, F.at(f"ds{c}", i))
                    for h in range(2):
                        ins = stt(state[:, (c + 1) % 2, h, :], state[:, c % 2, h, :], fcur[:, h, F_GL0 + par, t:t + 1],
                                  two("A")[:, 1, h * P:(h + 1) * P], ALU.mult, ALU.add)
                    ins.then_inc(region_free["A"], 1)
                    dv.drain().then_inc(s_done, 1)
                    if c < SCAN_SLOTS:
                        slot_scale(len(LEVELS) - 1 + c)
                    if t >= 1:
                        (outputs_norm if par else inverse_of_rows)(t - 1)
                inverse_of_rows(NT - 1)
                outputs_norm(NT - 1)
                for h in range(2):
                    dv.wait_ge(filled, F.at(f"ot{h}", i))
                dv.sem_inc(dve_turn, 1)

            dv.wait_ge(act_turn, PAIRS + 1)
            dv.sem_inc(merged, 2)
            with dv.Fori(0, KD // 2) as i:
                for b in range(2):
                    dv.wait_ge(gate_done, 2 * i + (b + 1))
                    dv.wait_ge(filled, MERGE_F.at("y0" if b == 0 else "yb1", i))
                    ya, yb = (two("B")[:, 0, :], two("B")[:, 1, :]) if b == 0 else (region("D", 512), region("E", 512))
                    ins = tt(mm_[:, 0, :], gs_[b][:, 0, :], ya)
                    if b == 1:
                        ins.then_inc(region_free["D"], 1)
                    tt(mm_[:, 1, :], gs_[b][:, 1, :], yb).then_inc(region_free["B" if b == 0 else "E"], 1)
                    dv.drain()
                    tt(mT[:, bass.ds(2 * i + b, 1), :].rearrange("p o s -> p (o s)"), mm_[:, 0, :], mm_[:, 1, :], ALU.add).then_inc(merged, 1)
                    dv.drain()

            dv.wait_ge(bias_ld, 32)
            for part in range(3):
                if part:
                    dv.wait_ge(bias_st, 16 * part)
                dv.tensor_copy(bpart, bfull)
                dv.drain().then_inc(bias_cast, 1)
                if part < 2:
                    tt(bfull, bfull, bpart, ALU.subtract)
                    dv.drain()
            dv.memset(ones3[:, :], 1.0).then_inc(ones3_done, 1)

            F = OUT_F
            dv.wait_ge(x2_in, 16 * NT)
            for t in range(NT):
                r = F.region[f"x{t}"]
                dv.wait_ge(filled, F.at(f"x{t}"))
                tt(x2[:, t, :], x2[:, t, :], region(r), ALU.add).then_inc(x2_done, 1)
                dv.drain().then_inc(region_free[r], 1)
            dv.wait_ge(ssx2, 1)
            inverse_mean(r4[:, 1, :], r4[:, 0, :], D).then_inc(inv2, 1)
            dv.wait_ge(rstd2, 1)
            dv.wait_ge(row_in, 16)
            for t in range(NT):
                stt(h2[:, t, :], x2[:, t, :], r4[:, 1, t:t + 1], nrow).then_inc(h2_done, 1)
            dv.wait_ge(filled, F.at("lt"))
            tt(lg, region("B")[:, 0:NT * NE].rearrange("p (t e) -> p t e", t=NT),
               br[:, :].unsqueeze(1).broadcast_to([P, NT, NE]), ALU.add).then_inc(region_free["B"], 1)
            dv.drain()
            for t in range(NT):
                dv.max(mx8[:, t, :], lg[:, t, :])
            dv.drain()
            for t in range(NT):
                dv.max_index(ix8[:, t, :], mx8[:, t, :], lg[:, t, :])
            tt(e4, mx8[:, :, 0:TOPK], mx8[:, :, 0:1].broadcast_to([P, NT, TOPK]), ALU.subtract).then_inc(dif_done, 1)
            dv.drain()
            dv.tensor_copy(ixf, ix8[:, :, 0:TOPK])
            dv.drain()
            tt(oh, sm[:, 0:NE].unsqueeze(1).broadcast_to([P, 16, NE]),
               ixf.rearrange("p t k -> p (t k)").unsqueeze(2).broadcast_to([P, 16, NE]), ALU.is_equal)
            dv.drain()
            dv.tensor_reduce(msk, oh.rearrange("p (t k) e -> p t e k", t=NT), AXX, ALU.add).then_inc(msk_done, 1)
            dv.wait_ge(e4_done, 1)
            dv.tensor_reduce(sum4[:, 0:NT], e4, AXX, ALU.add)
            dv.drain()
            dv.reciprocal(sum4[:, 4:4 + NT], sum4[:, 0:NT])
            dv.drain()
            tt(w4[:, :, :], e4, sum4[:, 4:4 + NT].unsqueeze(2).broadcast_to([P, NT, TOPK]))
            dv.wait_ge(filled, F.at("pos"))
            pos = region("C")[:, 0:NT * NE].rearrange("p (t e) -> p t e", t=NT)
            dv.tensor_scalar(bb, pos, float(P), None, ALU.is_ge)
            dv.drain()
            stt(bb, pos, float(2 * P), bb, ALU.is_ge, ALU.add)
            dv.drain()
            stt(bb, pos, float(3 * P), bb, ALU.is_ge, ALU.add)
            stt(adr, pos, float(P), sm[:, NE:2 * NE].unsqueeze(1).broadcast_to([P, NT, NE]), ALU.mult, ALU.add).then_inc(region_free["C"], 1)
            dv.drain()
            stt(adr, bb, 1.0 - P * P, adr, ALU.mult, ALU.add)
            dv.drain()
            for t in range(NT):
                tt(pk[:, TOPK * t:TOPK * (t + 1), :], oh[:, TOPK * t:TOPK * (t + 1), :],
                   adr[:, t, :].unsqueeze(1).broadcast_to([P, TOPK, NE]))
            dv.drain()
            dv.tensor_reduce(a16, pk, AXX, ALU.add)
            dv.drain()
            dv.tensor_copy(a16i, a16).then_inc(addr_done, 1)
            dv.wait_ge(filled, F.at("tot"))
            dv.tensor_copy(cnt[:, 0:1], region("D")[0:NE, 0:1]).then_inc(region_free["D"], 1)
            dv.drain()
            dv.tensor_scalar(fl[:, 0:3], thr[:, 0:3], cnt[:, 0:1], None, ALU.is_lt)
            dv.drain()
            dv.tensor_reduce(tot[:, 0:1], fl[:, 0:3], AXX, ALU.add).then_inc(cnt_done, 1)
            dv.wait_ge(filled, F.at("ex"))
            dv.tensor_copy(cnt[:, 1:2], region("E", 512)[0:NE, 0:1]).then_inc(region_free["E"], 1)
            dv.drain()
            dv.tensor_scalar(rk[:, 0:3], thr[:, 3:6], cnt[:, 1:2], None, ALU.add)
            dv.drain()
            oj3 = oj.rearrange("p (b j) -> p b j", b=3)
            tt(oj3, sm[0:NE, 2 * NE:2 * NE + 16].unsqueeze(1).broadcast_to([NE, 3, 16]),
               rk[:, 0:3].unsqueeze(2).broadcast_to([NE, 3, 16]), ALU.is_equal)
            dv.drain()
            tt(oj3, oj3, fl[:, 0:3].unsqueeze(2).broadcast_to([NE, 3, 16]))
            dv.drain()
            for n in range(2):
                tt(ol[:, 48 * n:48 * (n + 1)].rearrange("p (b j) -> p b j", b=3), oj3,
                   thr[:, 6 + 3 * n:9 + 3 * n].unsqueeze(2).broadcast_to([NE, 3, 16]))
            dv.tensor_copy(ol[:, 96:97], tot[:, 0:1])
            dv.drain().then_inc(list_src, 1)
            dv.wait_ge(filled, F.at("li"))
            li = region("A")[0:1, 0:97]
            dv.tensor_reduce(lsf[:, 0:32].rearrange("p (a j) -> p a j", a=2),
                             li[:, 0:96].rearrange("p (a b j) -> p a j b", a=2, b=3), AXX, ALU.add)
            dv.tensor_copy(lsf[:, 32:33], li[:, 96:97]).then_inc(region_free["A"], 1)
            dv.drain()
            dv.tensor_copy(lst[0:1, 0:33], lsf[:, 0:33]).then_inc(list_done, 1)
            dv.wait_ge(tab_in, 16)
            dv.tensor_scalar(tok[:, :], tab[:, :], 2, None, ALU.arith_shift_right).then_inc(tok_ready, 1)

            def expert(n):
                for half in range(2):
                    dv.wait_ge(chunk_used, 12 * n + 4 * (half + 1))
                    gu = region("AB"[half]).rearrange("p (f two) -> p two f", two=2)
                    dv.tensor_scalar(gb, gu[:, 0, :], LIMIT, None, ALU.min).then_inc(g_min, 1)
                    dv.tensor_scalar(ub, gu[:, 1, :], LIMIT, -LIMIT, ALU.min, ALU.max).then_inc(gu_free, 1)
                    dv.wait_ge(sg_done, 2 * n + (half + 1))
                    dv.wait_ge(gu_free, 2 * n + (half + 1))
                    stt(ub, ub, 1.0, gb, ALU.add, ALU.mult)
                    dv.drain()
                    tt(act[:, half, :], ub, sgm).then_inc(act_done, 1)

            with dv.Fori(0, NE) as n:
                expert(n)
            extra = dv.value_load(lst[0:1, 32:33], min_val=0, max_val=MAX_EXTRA)
            with dv.If(extra > 0):
                with dv.Fori(0, MAX_EXTRA) as j:
                    with dv.If(j < extra):
                        expert(j + NE)

            def finish(t):
                dv.wait_ge(ssf, t + 1)
                inverse_mean(r4[:, 1, t:t + 1], r4[:, 0, t:t + 1], D).then_inc(invf, 1)
                dv.wait_ge(rstdf, t + 1)
                dv.wait_ge(row_in, 32)
                stt(x2[:, t, :], x2[:, t, :], r4[:, 1, t:t + 1], nrow).then_inc(out_done, 1)

            for t in range(NT):
                dv.wait_ge(y_in[t], 16)
                for k in range(TOPK):
                    if k and t == NT - 1:
                        dv.wait_ge(last_y_in[k - 1], 16)
                    stt(x2[:, t, :], yin[t][:, k, :], w4[:, t, k:k + 1], x2[:, t, :], ALU.mult, ALU.add)
                    dv.drain()
                dv.drain().then_inc(sum_done, 1)
                if t:
                    finish(t - 1)
            finish(NT - 1)

        @block.gpsimd
        def _(po):
            po.memset(krp, 0.0).then_inc(zeroed, 1)
            po.memset(vnew, 0.0).then_inc(zeroed, 1)
            po.wait_ge(const_in, 16 * 16)
            po.sem_inc(pool_turn, 1)
            with po.Fori(0, PAIRS) as i:
                F = PAIR_F
                po.wait_ge(act_turn, i + 1)
                po.wait_ge(dve_turn, i + 1)
                po.wait_ge(lf_done, i + 1)
                for dst, m, v in ((sg, M_INCL, fcur[:, :, F_G, :]), (sa, M_ID, lf[:, 2]), (sbq, M_ID, lf[:, 3])):
                    for h in range(2):
                        ins = po.tensor_tensor(dst[:, NT * h:NT * (h + 1), :], mk[:, m, :].unsqueeze(1).broadcast_to([P, NT, P]),
                                               v[:, h, :].unsqueeze(2).broadcast_to([P, NT, P]), ALU.mult)
                    ins.then_inc(src_done, 1)
                po.wait_ge(lt_done, i + 1)
                for n in range(len(LEVELS) - 1):
                    if n:
                        po.wait_ge(filled, F.at(f"x{LEVELS[n]}", i))
                    po.tensor_tensor(cm, lt_, mk[:, M_LEVEL + 1 + n, :].unsqueeze(1).broadcast_to([P, 2 * NT, P]),
                                     ALU.mult).then_inc(cm_done, 1)
                po.wait_ge(cm_done, (len(LEVELS) - 1) * (i + 1))
                po.sem_inc(pool_turn, 1)

            po.wait_ge(filled, OUT_F.at("lt"))
            po.memset(xg, 0.0).then_inc(xg_clear, 1)
            po.wait_ge(addr_done, 1)
            po.wait_ge(table_clear, 16)
            for c in range(NT * TOPK):
                po.indirect_dma_start(out=slot_dram, out_offset=bass.IndirectOffsetOnAxis(ap=a16i[:, c:c + 1], axis=0),
                                      in_=valt[:, c:c + 1], in_offset=None, bounds_check=P * P - 1,
                                      oob_is_err=False).then_inc(table_set, 16)
            po.wait_ge(tok_ready, 1)
            po.wait_ge(h2_st, 16 * NT)
            po.wait_ge(xg_clear, 1)

            def wait_past(s, value):
                po.wait_ge(s, value)
                po.sem_inc(waits_passed, 1)

            def gather(n, q):
                if not first(n):
                    wait_past(xt_done, n)
                po.tensor_copy(gix[:, :], tok[:, bass.ds(q, 1)]).then_inc(gix_done, 1)
                wait_past(gix_done, n + 1)
                po.indirect_dma_start(out=xg, out_offset=None, in_=h2_dram,
                                      in_offset=bass.IndirectOffsetOnAxis(ap=gix[:, 0:1], axis=0),
                                      bounds_check=SEQ - 1, oob_is_err=False).then_inc(gathered, 16)

            def scatter(n, q):
                po.tensor_copy(six[:, :], tab[:, bass.ds(q, 1)]).then_inc(six_done, 1)
                po.wait_ge(six_done, n + 1)
                wait_past(ys_done, n + 1)
                po.indirect_dma_start(out=y_dram, out_offset=bass.IndirectOffsetOnAxis(ap=six[:, 0:1], axis=0),
                                      in_=ys, in_offset=None, bounds_check=SEQ * TOPK - 1,
                                      oob_is_err=False).then_inc(scattered, 16)

            gather(0, 0)
            gather(1, 4)
            scatter(0, 0)
            with po.Fori(1, NE - 1) as n:
                gather(n + 1, 4 * n + 4)
                wait_past(scattered, 16 * n)
                scatter(n, 4 * n)
            po.wait_ge(scattered, 16 * (NE - 1))
            scatter(NE - 1, 4 * (NE - 1))
            po.wait_ge(scattered, 16 * NE)
            extra = po.value_load(lst[0:1, 32:33], min_val=0, max_val=MAX_EXTRA)
            with po.If(extra > 0):
                with po.Fori(0, MAX_EXTRA) as j:
                    with po.If(j < extra):
                        q = po.value_load(lst[0:1, bass.ds(j, 1)], min_val=0, max_val=4 * NE - 1)
                        gather(j + NE, q)
                        scatter(j + NE, q)
                        wait_past(scattered, 16 * j + 16 * (NE + 1))
            po.sem_inc(all_rows, 1)


def constants():
    k, m = np.meshgrid(np.arange(P), np.arange(P), indexing="ij")
    same = k // CHUNK == m // CHUNK
    mats = [same & (k <= m), same, same | True, (k < CHUNK) & (m >= 0), (k >= CHUNK) & (m >= 0), k == m, k < m]
    mats += [(k // (2 * s) == m // (2 * s)) & (k % (2 * s) < s) & (m % (2 * s) >= s) for s in LEVELS]
    masks = np.stack([a.astype(np.float32) for a in mats], axis=1)
    diag = np.where((k < CHUNK) & (m >= CHUNK), np.float32(NEG), np.float32(0)).astype(np.float32)
    half = 1.0 / (np.float32(10000.0) ** (np.arange(0, ROPE, 2, dtype=np.float32) / np.float32(ROPE)))
    ang = np.arange(SEQ, dtype=np.float32)[None, :] * half.astype(np.float32)[:, None]
    c, s = np.cos(ang), np.sin(ang)
    cos = np.concatenate([c, c, c, c]).astype(np.float32)
    sin = np.concatenate([-s, s, -s, s]).astype(np.float32)
    small = np.zeros((P, 112), np.float32)
    small[:, 0:32] = np.arange(32)
    small[:, 32:64] = 4 * np.arange(32)
    small[:, 64:80] = np.arange(16)
    e = np.arange(NE)[:, None]
    small[0:NE, 96:99] = P * np.arange(1, 4)
    small[0:NE, 99:102] = np.arange(3)
    small[0:NE, 102:105] = 4 * e + np.arange(1, 4)
    small[0:NE, 105:108] = e
    ints = np.full((P, 144), FAR, np.int32)
    ints[:, 0:16] = (TOPK * (np.arange(P)[:, None, None] + P * np.arange(NT)[None, :, None])
                     + np.arange(TOPK)[None, None, :]).reshape(P, 16)
    return dict(masks=masks, diag=diag, cos=cos, sin=sin, small=small, ints=ints)


def kernel(x, norm_mix_w, w_in, gdn_conv_w, gdn_a_log, gdn_dt_bias, gdn_norm_w, w_gdn_o, mla_q_norm_w, w_mla_q_b,
           mla_kv_norm_w, w_mla_kv_b, w_mla_o, w_out, norm_ffn_w, w_router, b_router, w_gate_up, b_gate_up,
           w_down, b_down, norm_final_w):
    from concourse import bacc
    from concourse.bass_utils import run_bass_kernel_spmd

    def tiles(w):
        w = np.asarray(w)
        return w.reshape(-1, P, w.shape[-1]).transpose(1, 0, 2)

    def rows(v, n=P):
        return np.broadcast_to(np.asarray(v).reshape(1, -1), (n, np.asarray(v).size))

    w = np.asarray(w_in)[0]
    at = np.cumsum([0, 1024, 1024, 1024, 1024, 8, 8, Q_LORA, KV_LORA + ROPE, D, D])
    cq, ckv, ga, gb = (w[:, at[n]:at[n + 1]] for n in (6, 7, 8, 9))
    pair = np.stack([np.stack([tiles(w[:, 1024 * n + 256 * i:1024 * n + 256 * (i + 1)]) for n in range(4)]) for i in range(PAIRS)])
    conv = np.asarray(gdn_conv_w)[0].reshape(4, 3, PAIRS, 2, P)
    qb = np.asarray(w_mla_q_b)[0].reshape(Q_LORA, PAIRS, 2, 192)
    qb = np.stack([tiles(np.concatenate([qb[:, i, 0, :128], qb[:, i, 1, :128], qb[:, i, 0, 128:], qb[:, i, 1, 128:]], 1)) for i in range(PAIRS)])
    kvb = np.asarray(w_mla_kv_b)[0].reshape(KV_LORA, PAIRS, 2, 256)
    kvb = np.stack([tiles(np.concatenate([kvb[:, i, 0, :128], kvb[:, i, 1, :128], kvb[:, i, 0, 128:], kvb[:, i, 1, 128:]], 1)) for i in range(PAIRS)])
    four = [ga, gb, np.asarray(w_gdn_o)[0], np.asarray(w_mla_o)[0]]
    merge = np.stack([np.stack([tiles(m[:, P * j:P * (j + 1)]) for m in four], axis=1) for j in range(KD)])
    data = dict(
        x=np.asarray(x)[0], norm_mix=np.asarray(norm_mix_w)[0].reshape(KD, P).T, w_ba=tiles(w[:, at[4]:at[6]]),
        a_log=rows(gdn_a_log), dt_bias=rows(gdn_dt_bias), w_cq=tiles(cq),
        w_ckv=tiles(np.concatenate([ckv, ckv[:, KV_LORA:]], 1)), q_norm=np.asarray(mla_q_norm_w)[0].reshape(KQ, P).T,
        kv_norm=np.asarray(mla_kv_norm_w)[0].reshape(KKV, P).T, w_pair=pair,
        conv_w=conv.transpose(4, 2, 1, 3, 0).reshape(P, PAIRS, 24), w_qb=qb, w_kvb=kvb, gdn_norm=rows(gdn_norm_w),
        w_merge=merge, w_out=np.stack([tiles(np.asarray(w_out)[0][:, 512 * h:512 * (h + 1)]) for h in range(2)]),
        norm_ffn=np.asarray(norm_ffn_w), w_router=tiles(np.asarray(w_router)[0]), b_router=rows(b_router),
        w_gu=np.asarray(w_gate_up)[0], b_gu=np.asarray(b_gate_up)[0], w_dn=np.asarray(w_down)[0],
        b_dn=np.asarray(b_down)[0], norm_final=np.asarray(norm_final_w)[None, :], **constants())
    nc = bacc.Bacc("TRN2", target_bir_lowering=False, num_devices=1)
    args = {}
    for name, a in data.items():
        data[name] = a = np.ascontiguousarray(a)
        args[name] = nc.dram_tensor("in_" + name, a.shape, mybir.dt.from_np(a.dtype), kind="ExternalInput").ap()
    out = nc.dram_tensor("out", (SEQ, D), F32, kind="ExternalOutput").ap()
    build(nc, out=out, **args)
    r = run_bass_kernel_spmd(nc, [{"in_" + n: a for n, a in data.items()}], core_ids=[0])
    return r.results[0]["out"].reshape(1, SEQ, D)
```
